# Optimizing a Trainium2 kernel written in Bass

```python
import math
import jax, jax.numpy as jnp
from jax import lax
import numpy as np

D_MODEL = 1024
BATCH = 1
SEQ = 256
DEPTH = 1

MEM_LEN = 256
EPS = 1e-6
CHUNK = 64

SSD_D_INNER = D_MODEL
SSD_HEAD_DIM = 64
SSD_HEADS = SSD_D_INNER // SSD_HEAD_DIM
SSD_GROUPS = 2
SSD_STATE = 128
SSD_CONV = 4
SSD_CONV_CH = SSD_D_INNER + 2 * SSD_GROUPS * SSD_STATE
DT_MIN = 1e-3
DT_MAX = 1e-1

GLA_HEADS = 4
GLA_DK = D_MODEL // 2
GLA_DV = D_MODEL
GLA_HEAD_K = GLA_DK // GLA_HEADS
GLA_HEAD_V = GLA_DV // GLA_HEADS
GLA_GATE_RANK = 16
GLA_TAU = 16.0

XATTN_HEADS = 4
XATTN_HEAD_DIM = D_MODEL // XATTN_HEADS

D_FF = -((-8 * D_MODEL) // (3 * 256)) * 256

IN_SIZES = (SSD_D_INNER, SSD_CONV_CH, SSD_HEADS,
            GLA_DK, GLA_DK, GLA_DV, GLA_DV, GLA_GATE_RANK,
            D_MODEL, D_MODEL)
IN_WIDTH = sum(IN_SIZES)


def rmsnorm(x, g):
    xf = x.astype(jnp.float32)
    y = xf * lax.rsqrt(jnp.mean(xf * xf, axis=-1, keepdims=True) + EPS)
    return (y * g.astype(jnp.float32)).astype(x.dtype)

def causal_dwconv(x, w, b):
    y = lax.conv_general_dilated(x, w, window_strides=(1,), padding=[(SSD_CONV - 1, 0)],
                                 dimension_numbers=('NWC', 'WIO', 'NWC'),
                                 feature_group_count=x.shape[-1])
    return y + b

def segsum_exp(a):
    L = a.shape[-1]
    cs = jnp.cumsum(a, axis=-1)
    mask = jnp.tril(jnp.ones((L, L), dtype=bool))
    diff = cs[..., :, None] - cs[..., None, :]
    return jnp.where(mask, jnp.exp(jnp.where(mask, diff, 0.0)), 0.0)

def ssd_mixer(z, xBC, dt_raw, conv_w, conv_b, dt_bias, A_log, D_skip, norm_g):
    Bsz, S, _ = z.shape
    nc = S // CHUNK
    G, R, P, N = SSD_GROUPS, SSD_HEADS // SSD_GROUPS, SSD_HEAD_DIM, SSD_STATE
    xBC = jax.nn.silu(causal_dwconv(xBC, conv_w, conv_b)).astype(jnp.float32)
    xs, Bm, Cm = jnp.split(xBC, [SSD_D_INNER, SSD_D_INNER + G * N], axis=-1)
    dt = jax.nn.softplus(dt_raw.astype(jnp.float32) + dt_bias.astype(jnp.float32))
    A = -jnp.exp(A_log.astype(jnp.float32))
    x_heads = xs.reshape(Bsz, S, SSD_HEADS, P)
    X = (x_heads * dt[..., None]).reshape(Bsz, nc, CHUNK, G, R, P)
    a = (dt * A).reshape(Bsz, nc, CHUNK, G, R).transpose(0, 3, 4, 1, 2)
    Bc = Bm.reshape(Bsz, nc, CHUNK, G, N)
    Cc = Cm.reshape(Bsz, nc, CHUNK, G, N)
    a_cs = jnp.cumsum(a, axis=-1)
    Lmat = segsum_exp(a)
    CB = jnp.einsum('bclgn,bcsgn->bcgls', Cc, Bc)
    y_diag = jnp.einsum('bcgls,bgrcls,bcsgrp->bclgrp', CB, Lmat, X)
    decay_states = jnp.exp(a_cs[..., -1:] - a_cs)
    states = jnp.einsum('bclgn,bgrcl,bclgrp->bcgrpn', Bc, decay_states, X)
    chunk_decay = jnp.exp(a_cs[..., -1])

    def chunk_step(state, inp):
        st_c, dec_c = inp
        return state * dec_c[..., None, None] + st_c, state

    init = jnp.zeros((Bsz, G, R, P, N), jnp.float32)
    _, prev = lax.scan(chunk_step, init, (jnp.moveaxis(states, 1, 0), jnp.moveaxis(chunk_decay, 3, 0)))
    prev = jnp.moveaxis(prev, 0, 1)
    y_off = jnp.einsum('bclgn,bcgrpn,bgrcl->bclgrp', Cc, prev, jnp.exp(a_cs))
    y = (y_diag + y_off).reshape(Bsz, S, SSD_HEADS, P) + D_skip.astype(jnp.float32)[:, None] * x_heads
    y = y.reshape(Bsz, S, SSD_D_INNER) * jax.nn.silu(z.astype(jnp.float32))
    y = rmsnorm(y.reshape(Bsz, S, G, SSD_D_INNER // G), norm_g.reshape(G, SSD_D_INNER // G))
    return y.reshape(Bsz, S, SSD_D_INNER).astype(z.dtype)

def gla_mixer(q, k, v, r, a1, w_a2, b_a, norm_g):
    Bsz, S, _ = q.shape
    nc = S // CHUNK
    H, dk, dv = GLA_HEADS, GLA_HEAD_K, GLA_HEAD_V
    log_alpha = jax.nn.log_sigmoid((a1 @ w_a2 + b_a).astype(jnp.float32)) / GLA_TAU
    qc = q.astype(jnp.float32).reshape(Bsz, nc, CHUNK, H, dk) * (dk ** -0.5)
    kc = k.astype(jnp.float32).reshape(Bsz, nc, CHUNK, H, dk)
    vc = v.astype(jnp.float32).reshape(Bsz, nc, CHUNK, H, dv)
    bcum = jnp.cumsum(log_alpha.reshape(Bsz, nc, CHUNK, H, dk), axis=2)
    b_last = bcum[:, :, -1:]
    q_t = qc * jnp.exp(bcum)
    k_t = kc * jnp.exp(-bcum)
    k_h = kc * jnp.exp(b_last - bcum)
    mask = jnp.tril(jnp.ones((CHUNK, CHUNK), dtype=bool))
    att = jnp.where(mask, jnp.einsum('bclhd,bcshd->bchls', q_t, k_t), 0.0)
    o_intra = jnp.einsum('bchls,bcshv->bclhv', att, vc)
    U = jnp.einsum('bclhd,bclhv->bchdv', k_h, vc)
    dec = jnp.exp(b_last[:, :, 0])

    def chunk_step(state, inp):
        u_c, d_c = inp
        return state * d_c[..., None] + u_c, state

    init = jnp.zeros((Bsz, H, dk, dv), jnp.float32)
    _, prev = lax.scan(chunk_step, init, (jnp.moveaxis(U, 1, 0), jnp.moveaxis(dec, 1, 0)))
    prev = jnp.moveaxis(prev, 0, 1)
    o_inter = jnp.einsum('bclhd,bchdv->bclhv', q_t, prev)
    o = (o_intra + o_inter).reshape(Bsz, S, H, dv)
    o = rmsnorm(o, norm_g).reshape(Bsz, S, GLA_DV)
    return (o * jax.nn.silu(r.astype(jnp.float32))).astype(q.dtype)

def hybrid_mixer(n, w_in, conv_w, conv_b, dt_bias, A_log, D_skip, ssd_norm,
                 gla_w_a2, gla_b_a, gla_norm, w_up_ssd, w_up_gla, w_o):
    proj = n @ w_in
    idx = np.cumsum(IN_SIZES)[:-1].tolist()
    z, xBC, dt_raw, q, k, v, r, a1, g_ssd, g_gla = jnp.split(proj, idx, axis=-1)
    y_ssd = ssd_mixer(z, xBC, dt_raw, conv_w, conv_b, dt_bias, A_log, D_skip, ssd_norm)
    y_gla = gla_mixer(q, k, v, r, a1, gla_w_a2, gla_b_a, gla_norm)
    merged = jax.nn.sigmoid(g_ssd) * (y_ssd @ w_up_ssd) + jax.nn.sigmoid(g_gla) * (y_gla @ w_up_gla)
    return merged @ w_o

def mem_cross_attention(n, m, w_xq, w_xkv, w_xo):
    Bsz, S, _ = n.shape
    q = (n @ w_xq).reshape(Bsz, S, XATTN_HEADS, XATTN_HEAD_DIM)
    k, v = jnp.split(m @ w_xkv, 2, axis=-1)
    k = k.reshape(Bsz, -1, XATTN_HEADS, XATTN_HEAD_DIM)
    v = v.reshape(Bsz, -1, XATTN_HEADS, XATTN_HEAD_DIM)
    s = jnp.einsum('bshd,bmhd->bhsm', q, k).astype(jnp.float32) * (XATTN_HEAD_DIM ** -0.5)
    p = jax.nn.softmax(s, axis=-1).astype(v.dtype)
    o = jnp.einsum('bhsm,bmhd->bshd', p, v).reshape(Bsz, S, D_MODEL)
    return o @ w_xo

def swiglu(n, w_ffn_in, w_ffn_out):
    g, u = jnp.split(n @ w_ffn_in, 2, axis=-1)
    return (jax.nn.silu(g) * u) @ w_ffn_out

def first_inputs(seed: int = 0) -> dict:
    key = jax.random.key(seed)
    ks = jax.random.split(key, 26)
    f32 = jnp.float32
    L = DEPTH

    def nrm(k, shape, scale):
        return jax.random.normal(k, shape, f32) * scale

    def gain(k, shape):
        return 1.0 + 0.02 * jax.random.normal(k, shape, f32)

    dt = jnp.exp(jax.random.uniform(ks[6], (L, SSD_HEADS), f32, math.log(DT_MIN), math.log(DT_MAX)))
    dt_bias = dt + jnp.log(-jnp.expm1(-dt))
    A_log = jnp.log(jax.random.uniform(ks[7], (L, SSD_HEADS), f32, 1.0, 16.0))
    return {
        "x": jax.random.normal(ks[0], (BATCH, SEQ, D_MODEL), f32),
        "mem": jax.random.normal(ks[1], (BATCH, MEM_LEN, D_MODEL), f32),
        "norm_mix": gain(ks[2], (L, D_MODEL)),
        "w_in": nrm(ks[3], (L, D_MODEL, IN_WIDTH), D_MODEL ** -0.5),
        "ssd_conv_w": nrm(ks[4], (L, SSD_CONV, 1, SSD_CONV_CH), SSD_CONV ** -0.5),
        "ssd_conv_b": nrm(ks[5], (L, SSD_CONV_CH), 0.02),
        "ssd_dt_bias": dt_bias,
        "ssd_A_log": A_log,
        "ssd_D": 1.0 + 0.1 * jax.random.normal(ks[8], (L, SSD_HEADS), f32),
        "ssd_norm": gain(ks[9], (L, SSD_D_INNER)),
        "gla_w_a2": nrm(ks[10], (L, GLA_GATE_RANK, GLA_DK), GLA_GATE_RANK ** -0.5),
        "gla_b_a": nrm(ks[11], (L, GLA_DK), 0.02),
        "gla_norm": gain(ks[12], (L, GLA_HEAD_V)),
        "w_up_ssd": nrm(ks[13], (L, SSD_D_INNER, D_MODEL), SSD_D_INNER ** -0.5),
        "w_up_gla": nrm(ks[14], (L, GLA_DV, D_MODEL), GLA_DV ** -0.5),
        "w_o": nrm(ks[15], (L, D_MODEL, D_MODEL), D_MODEL ** -0.5),
        "norm_xattn": gain(ks[16], (L, D_MODEL)),
        "norm_mem": gain(ks[17], (L, D_MODEL)),
        "w_xq": nrm(ks[18], (L, D_MODEL, D_MODEL), D_MODEL ** -0.5),
        "w_xkv": nrm(ks[19], (L, D_MODEL, 2 * D_MODEL), D_MODEL ** -0.5),
        "w_xo": nrm(ks[20], (L, D_MODEL, D_MODEL), D_MODEL ** -0.5),
        "norm_ffn": gain(ks[21], (L, D_MODEL)),
        "w_ffn_in": nrm(ks[22], (L, D_MODEL, 2 * D_FF), D_MODEL ** -0.5),
        "w_ffn_out": nrm(ks[23], (L, D_FF, D_MODEL), D_FF ** -0.5),
        "norm_final": gain(ks[24], (D_MODEL,)),
    }

def first_block(x, mem, norm_mix, w_in, ssd_conv_w, ssd_conv_b, ssd_dt_bias, ssd_A_log, ssd_D, ssd_norm,
              gla_w_a2, gla_b_a, gla_norm, w_up_ssd, w_up_gla, w_o, norm_xattn, norm_mem, w_xq, w_xkv,
              w_xo, norm_ffn, w_ffn_in, w_ffn_out, norm_final):
    h = x
    for i in range(DEPTH):
        h = h + hybrid_mixer(rmsnorm(h, norm_mix[i]), w_in[i], ssd_conv_w[i], ssd_conv_b[i], ssd_dt_bias[i],
                             ssd_A_log[i], ssd_D[i], ssd_norm[i], gla_w_a2[i], gla_b_a[i], gla_norm[i],
                             w_up_ssd[i], w_up_gla[i], w_o[i])
        h = h + mem_cross_attention(rmsnorm(h, norm_xattn[i]), rmsnorm(mem, norm_mem[i]),
                                    w_xq[i], w_xkv[i], w_xo[i])
        h = h + swiglu(rmsnorm(h, norm_ffn[i]), w_ffn_in[i], w_ffn_out[i])
    return rmsnorm(h, norm_final)


DEPTH_2 = 2

Q_BLOCK = 128
N_MIXERS = 2
N_MLA_LAYERS = (DEPTH_2 + 1) // 2
N_FOX_LAYERS = DEPTH_2 // 2
D_FF_2 = 256 * ((8 * D_MODEL // 3 + 255) // 256)
PLE_DIM = 256
MLA_HEADS = 8
MLA_NOPE = 128
MLA_ROPE = 64
MLA_V = 128
MLA_Q_LORA = 256
MLA_KV_LORA = 128
ROPE_THETA = 10000.0
FOX_HEADS = 8
FOX_HEAD_DIM = 128
NORM_EPS = 1e-6
NEG_INF = -1e30


def rms_norm(x, g):
    xf = x.astype(jnp.float32)
    y = xf * lax.rsqrt(jnp.mean(xf * xf, axis=-1, keepdims=True) + NORM_EPS)
    return (y * g.astype(jnp.float32)).astype(x.dtype)

def swiglu_2(x, w_in, w_out):
    gate, up = jnp.split(x @ w_in, 2, axis=-1)
    return (jax.nn.silu(gate) * up) @ w_out

def apply_rope(x, cos, sin):
    x1, x2 = jnp.split(x, 2, axis=-1)
    return jnp.concatenate([x1 * cos - x2 * sin, x2 * cos + x1 * sin], axis=-1)

def causal_block_attention(scores_fn, v, chunk_causal):
    seq = v.shape[1]
    outs = []
    for q0 in range(0, seq, Q_BLOCK):
        q1 = q0 + Q_BLOCK
        s = scores_fn(q0, q1)
        q_pos = jnp.arange(q0, q1)
        k_pos = jnp.arange(q1)
        if chunk_causal:
            allowed = (k_pos[None, :] // CHUNK) <= (q_pos[:, None] // CHUNK)
        else:
            allowed = k_pos[None, :] <= q_pos[:, None]
        s = jnp.where(allowed, s, NEG_INF)
        probs = jax.nn.softmax(s, axis=-1).astype(v.dtype)
        outs.append(jnp.einsum('bhqk,bkhd->bqhd', probs, v[:, :q1]))
    return jnp.concatenate(outs, axis=1)

def mla_mixer(u, cos, sin, w_down, q_norm, w_uq, kv_norm, w_ukv, w_o):
    b, s, _ = u.shape
    c = u @ w_down
    c_q, c_kv, k_rope = jnp.split(c, [MLA_Q_LORA, MLA_Q_LORA + MLA_KV_LORA], axis=-1)
    q = (rms_norm(c_q, q_norm) @ w_uq).reshape(b, s, MLA_HEADS, MLA_NOPE + MLA_ROPE)
    q_nope, q_rope = jnp.split(q, [MLA_NOPE], axis=-1)
    q_rope = apply_rope(q_rope, cos[:, :, None, :], sin[:, :, None, :])
    k_rope = apply_rope(k_rope, cos, sin)
    kv = (rms_norm(c_kv, kv_norm) @ w_ukv).reshape(b, s, MLA_HEADS, MLA_NOPE + MLA_V)
    k_nope, v = jnp.split(kv, [MLA_NOPE], axis=-1)
    scale = (MLA_NOPE + MLA_ROPE) ** -0.5

    def scores(q0, q1):
        sc = (jnp.einsum('bqhd,bkhd->bhqk', q_nope[:, q0:q1], k_nope[:, :q1])
              + jnp.einsum('bqhr,bkr->bhqk', q_rope[:, q0:q1], k_rope[:, :q1]))
        return sc.astype(jnp.float32) * scale

    o = causal_block_attention(scores, v, chunk_causal=True)
    return o.reshape(b, s, MLA_HEADS * MLA_V) @ w_o

def fox_mixer(u, w_in, b_f, w_o):
    b, s, _ = u.shape
    hd = FOX_HEADS * FOX_HEAD_DIM
    proj = u @ w_in
    q, k, v, f_logit = jnp.split(proj, [hd, 2 * hd, 3 * hd], axis=-1)
    q = q.reshape(b, s, FOX_HEADS, FOX_HEAD_DIM)
    k = k.reshape(b, s, FOX_HEADS, FOX_HEAD_DIM)
    v = v.reshape(b, s, FOX_HEADS, FOX_HEAD_DIM)
    log_f = jax.nn.log_sigmoid(f_logit.astype(jnp.float32) + b_f.astype(jnp.float32))
    cum = jnp.cumsum(log_f, axis=1).transpose(0, 2, 1)
    scale = FOX_HEAD_DIM ** -0.5

    def scores(q0, q1):
        sc = jnp.einsum('bqhd,bkhd->bhqk', q[:, q0:q1], k[:, :q1]).astype(jnp.float32) * scale
        return sc + cum[:, :, q0:q1, None] - cum[:, :, None, :q1]

    o = causal_block_attention(scores, v, chunk_causal=False)
    return o.reshape(b, s, hd) @ w_o

def second_inputs(seed: int = 0) -> dict:
    key = jax.random.key(seed)
    ks = jax.random.split(key, 20)
    f32 = jnp.float32

    def dense(k, shape, fan_in):
        return jax.random.normal(k, shape, f32) * (fan_in ** -0.5)

    def gain(k, shape):
        return 1.0 + 0.05 * jax.random.normal(k, shape, f32)

    x = jax.random.normal(ks[0], (BATCH, SEQ, D_MODEL), f32)
    p = jax.random.normal(ks[1], (DEPTH_2, BATCH, SEQ, PLE_DIM), f32)
    offset = jax.random.randint(ks[2], (BATCH, 1), 0, 4096, dtype=jnp.int32)
    positions = (offset + jnp.arange(SEQ, dtype=jnp.int32)[None, :]).astype(jnp.int32)

    ffn_norm = gain(ks[3], (DEPTH_2, 2, D_MODEL))
    ffn_w_in = dense(ks[4], (DEPTH_2, 2, D_MODEL, 2 * D_FF_2), D_MODEL)
    ffn_w_out = dense(ks[5], (DEPTH_2, 2, D_FF_2, D_MODEL), D_FF_2)
    mix_norm = gain(ks[6], (DEPTH_2, D_MODEL))

    mla_w_down = dense(ks[7], (N_MLA_LAYERS, D_MODEL, MLA_Q_LORA + MLA_KV_LORA + MLA_ROPE), D_MODEL)
    mla_q_norm = gain(ks[8], (N_MLA_LAYERS, MLA_Q_LORA))
    mla_w_uq = dense(ks[9], (N_MLA_LAYERS, MLA_Q_LORA, MLA_HEADS * (MLA_NOPE + MLA_ROPE)), MLA_Q_LORA)
    mla_kv_norm = gain(ks[10], (N_MLA_LAYERS, MLA_KV_LORA))
    mla_w_ukv = dense(ks[11], (N_MLA_LAYERS, MLA_KV_LORA, MLA_HEADS * (MLA_NOPE + MLA_V)), MLA_KV_LORA)
    mla_w_o = dense(ks[12], (N_MLA_LAYERS, MLA_HEADS * MLA_V, D_MODEL), MLA_HEADS * MLA_V)

    fox_hd = FOX_HEADS * FOX_HEAD_DIM
    fox_w_in = dense(ks[13], (N_FOX_LAYERS, D_MODEL, 3 * fox_hd + FOX_HEADS), D_MODEL)
    fox_w_in = fox_w_in.at[..., 3 * fox_hd:].multiply(0.1)
    fox_b_f = jax.random.uniform(ks[14], (N_FOX_LAYERS, FOX_HEADS), f32, minval=1.0, maxval=6.0)
    fox_w_o = dense(ks[15], (N_FOX_LAYERS, fox_hd, D_MODEL), fox_hd)

    ple_norm = gain(ks[16], (DEPTH_2, D_MODEL))
    ple_w_gate = dense(ks[17], (DEPTH_2, D_MODEL, D_MODEL), D_MODEL)
    ple_w_proj = dense(ks[18], (DEPTH_2, PLE_DIM, D_MODEL), PLE_DIM)
    final_norm = gain(ks[19], (D_MODEL,))

    return {"x": x, "p": p, "positions": positions,
            "ffn_norm": ffn_norm, "ffn_w_in": ffn_w_in, "ffn_w_out": ffn_w_out,
            "mix_norm": mix_norm,
            "mla_w_down": mla_w_down, "mla_q_norm": mla_q_norm, "mla_w_uq": mla_w_uq,
            "mla_kv_norm": mla_kv_norm, "mla_w_ukv": mla_w_ukv, "mla_w_o": mla_w_o,
            "fox_w_in": fox_w_in, "fox_b_f": fox_b_f, "fox_w_o": fox_w_o,
            "ple_norm": ple_norm, "ple_w_gate": ple_w_gate, "ple_w_proj": ple_w_proj,
            "final_norm": final_norm}

def second_block(x, p, positions, ffn_norm, ffn_w_in, ffn_w_out, mix_norm,
              mla_w_down, mla_q_norm, mla_w_uq, mla_kv_norm, mla_w_ukv, mla_w_o,
              fox_w_in, fox_b_f, fox_w_o, ple_norm, ple_w_gate, ple_w_proj, final_norm):
    inv_freq = ROPE_THETA ** (-jnp.arange(0, MLA_ROPE, 2, dtype=jnp.float32) / MLA_ROPE)
    ang = positions.astype(jnp.float32)[..., None] * inv_freq
    cos = jnp.cos(ang).astype(x.dtype)
    sin = jnp.sin(ang).astype(x.dtype)

    h = x
    for i in range(DEPTH_2):
        h = h + 0.5 * swiglu_2(rms_norm(h, ffn_norm[i, 0]), ffn_w_in[i, 0], ffn_w_out[i, 0])
        u = rms_norm(h, mix_norm[i])
        j = i // N_MIXERS
        if i % N_MIXERS == 0:
            h = h + mla_mixer(u, cos, sin, mla_w_down[j], mla_q_norm[j], mla_w_uq[j],
                              mla_kv_norm[j], mla_w_ukv[j], mla_w_o[j])
        else:
            h = h + fox_mixer(u, fox_w_in[j], fox_b_f[j], fox_w_o[j])
        h = h + 0.5 * swiglu_2(rms_norm(h, ffn_norm[i, 1]), ffn_w_in[i, 1], ffn_w_out[i, 1])
        gate = jax.nn.sigmoid(rms_norm(h, ple_norm[i]) @ ple_w_gate[i])
        h = h + gate * (p[i] @ ple_w_proj[i])
    return rms_norm(h, final_norm)


def setup_inputs(seed=0):
    out = dict(first_inputs(seed))
    for name, value in second_inputs(seed + 1).items():
        if name != "x":
            out[name + "_2"] = value
    return out


def reference(
    x, mem, norm_mix, w_in, ssd_conv_w, ssd_conv_b, ssd_dt_bias, ssd_A_log, ssd_D, ssd_norm,
    gla_w_a2, gla_b_a, gla_norm, w_up_ssd, w_up_gla, w_o, norm_xattn, norm_mem, w_xq, w_xkv,
    w_xo, norm_ffn, w_ffn_in, w_ffn_out, norm_final, p_2, positions_2, ffn_norm_2, ffn_w_in_2,
    ffn_w_out_2, mix_norm_2, mla_w_down_2, mla_q_norm_2, mla_w_uq_2, mla_kv_norm_2, mla_w_ukv_2,
    mla_w_o_2, fox_w_in_2, fox_b_f_2, fox_w_o_2, ple_norm_2, ple_w_gate_2, ple_w_proj_2,
    final_norm_2,
):
    x = first_block(
        x, mem, norm_mix, w_in, ssd_conv_w, ssd_conv_b, ssd_dt_bias, ssd_A_log, ssd_D, ssd_norm,
        gla_w_a2, gla_b_a, gla_norm, w_up_ssd, w_up_gla, w_o, norm_xattn, norm_mem, w_xq, w_xkv,
        w_xo, norm_ffn, w_ffn_in, w_ffn_out, norm_final,
    )
    return second_block(
        x, p_2, positions_2, ffn_norm_2, ffn_w_in_2, ffn_w_out_2, mix_norm_2, mla_w_down_2,
        mla_q_norm_2, mla_w_uq_2, mla_kv_norm_2, mla_w_ukv_2, mla_w_o_2, fox_w_in_2, fox_b_f_2,
        fox_w_o_2, ple_norm_2, ple_w_gate_2, ple_w_proj_2, final_norm_2,
    )


_drawn_inputs = setup_inputs


def setup_inputs(seed=0):
    import zlib

    import numpy as np

    out = dict(_drawn_inputs(seed))
    spreads = {}
    factors = {'ssd_conv_b': 3.695,
     'ssd_norm': 5.501,
     'gla_b_a': 8.0,
     'gla_norm': 8.0,
     'norm_xattn': 8.0,
     'norm_mem': 8.0,
     'norm_ffn': 4.16,
     'norm_final': 2.784,
     'mix_norm_2': 2.757,
     'mla_q_norm_2': 8.0,
     'mla_kv_norm_2': 4.934,
     'ple_norm_2': 28.191}
    for name, (base, spread) in spreads.items():
        noise = np.random.default_rng([zlib.crc32(name.encode()), seed]).standard_normal(out[name].shape)
        drawn = base * np.exp(spread * noise) if base else spread * noise
        out[name] = __import__('jax').numpy.asarray(drawn.astype(out[name].dtype))
    for name, factor in factors.items():
        out[name] = (out[name] * factor).astype(out[name].dtype)
    return out
```

```python
from contextlib import ExitStack

import numpy as np

import concourse.bass as bass
from concourse import mybir

ALU = mybir.AluOpType
ACT = mybir.ActivationFunctionType
AX = mybir.AxisListType
F32 = mybir.dt.float32
F32R = mybir.dt.float32r
I32 = mybir.dt.int32
U32 = mybir.dt.uint32

P = 128
S = 256
NT = S // P
D = 1024
KD = D // P
EPS = 1e-6
CHUNK = 64
GROUP = 2048
RING = 3

SSD_HEADS, SSD_P, SSD_CH = 16, 64, 1536
GLA_HEADS, GLA_DK, GLA_DV, GLA_RANK, GLA_TAU = 4, 128, 256, 16, 16.0
X_HEADS, X_DH = 4, 256
D_FF = 2816
FB = 256
NJ = D_FF // FB
MLA_HEADS, NOPE, ROPE = 8, 128, 64
Q_LORA, KV_LORA = 256, 128
FOX_HEADS, FOX_DH = 8, 128
PLE_DIM = 256
N_FFN = 5

Z0, XBC0, DT0, Q0, K0, V0, R0, A10, GS0, GG0 = 0, 1024, 2560, 2576, 3088, 3600, 4624, 5648, 5664, 6688

T_ID, T_TRI, T_OU, T_CHUNK, T_CAUSAL, T_GLA, T_FREQ, T_END = 0, 128, 384, 640, 1024, 1408, 1536, 1568

C_NORM, C_FINAL, C_CONVW, C_CONVB, C_BA, C_QN, C_KVN, C_SSDN, C_GLAN, C_END = 0, 96, 104, 152, 164, 168, 170, 171, 179, 181
GAIN_AT = [0, 1, 2, 3, 4, 8, 5, 10, 6, 9, 7, 11]

MAGIC = 12582912.0
TWO_PI = (6.28125, 0.0019350051879882812, 3.01991598e-07)


def tables():
    i = np.arange(P)
    t = np.zeros((P, T_END), np.float32)
    t[:, T_ID:T_ID + P] = np.eye(P)
    t[:, T_TRI:T_TRI + P] = i[:, None] <= i[None, :]
    t[:, T_TRI + P:T_TRI + 2 * P] = 1.0
    t[:, T_OU:T_OU + P] = 1.0
    t[:, T_OU + P:T_OU + 2 * P] = i[:, None] > i[None, :]
    chunk = np.where(i[None, :] // CHUNK <= i[:, None] // CHUNK, 0.0, -1e30)
    causal = np.where(i[None, :] <= i[:, None], 0.0, -1e30)
    for at, m in ((T_CHUNK, chunk), (T_CAUSAL, causal)):
        t[:, at:at + P] = m
        t[:, at + 2 * P:at + 3 * P] = m
    t[:, T_GLA:T_GLA + P] = (i[:, None] <= i[None, :]) & (i[:, None] // CHUNK == i[None, :] // CHUNK)
    t[:, T_FREQ:T_FREQ + 32] = np.float32(10000.0) ** (-np.arange(0, ROPE, 2, dtype=np.float32) / np.float32(ROPE))
    return t


def lay_out():
    use, first, freed, cols = {}, {}, [], []
    full = [0] * 8
    used = 0

    def bank(key, b, n=1):
        use[key] = (b, full[b])
        full[b] += n

    def group(key, width):
        first.setdefault(key, len(freed))
        cols.append(width)
        freed.append(None)
        return len(freed) - 1

    def free_by_count(g):
        nonlocal used
        used += 1
        freed[g] = ("used", used)

    def free_by_bank(g, b):
        freed[g] = ("bank", b, full[b])

    def dense(name, pair, width=512):
        a = group(name, 4 * width)
        b = group(name, 4 * width)
        bank((name, 0), 2 * pair)
        bank((name, 1), 2 * pair + 1)
        free_by_count(a)
        free_by_bank(b, 2 * pair + 1)

    def banks(name, bs):
        for q, b in enumerate(bs):
            bank((name, q), b)

    def norm(n):
        banks(f"norm{n}", (4, 5, 6, 7))

    def ffn(n):
        first[f"ffn{n}"] = g0 = len(freed)
        for _ in range(3 * NJ):
            group(f"ffn{n}", GROUP)
        base0, base1 = full[0], full[1]
        bank((f"gu{n}", 0), 0, NJ)
        bank((f"gu{n}", 1), 1, NJ)
        bank((f"ht{n}", 0), 2, NJ)
        banks(f"acc{n}", (4, 5, 6, 7))
        nonlocal used
        first[f"ffn{n}_used"] = used
        freed[g0] = ("used", used + 1)
        freed[g0 + 1] = ("bank", 1, base1 + 1)
        used += 1
        for i in range(1, NJ):
            freed[g0 + 3 * i - 1] = ("used", used + 1)
            freed[g0 + 3 * i] = ("bank", 1, base1 + i + 1)
            freed[g0 + 3 * i + 1] = ("used", used + 2)
            used += 2
        freed[g0 + 3 * NJ - 1] = ("bank", 7, full[7])

    banks("cols", (3, 2, 0))
    norm(0)
    banks("small0", (3,))
    banks("a1t", (3,))
    dense("xbc0", 0)
    dense("xbc1", 1)
    banks("la", (4, 5))
    dense("xbc2", 0)
    dense("q", 1)
    dense("k", 0)
    banks("cbt", (6, 7))
    banks("xt", (4, 5, 6, 7))
    dense("v0", 1)
    dense("v1", 0)
    dense("r0", 1)
    dense("r1", 0)
    banks("att", (4, 5, 6, 7))
    dense("z0", 1)
    banks("glao", (4, 5, 6, 7))
    dense("z1", 0)
    for hg in range(4):
        for h in range(4):
            bank(("ssd_d", 4 * hg + h), 4 + h)
        dense(("gs0", "gs1", "gg0", "gg1")[hg], 0)
        if hg in (1, 2):
            for q in (0, 1):
                bank(("ygt", 2 * (hg - 1) + q), 2 + q)
        bank(("ssd_y", hg), 2 + hg % 2)
    dense("ugla0", 0)
    dense("ugla1", 1)
    banks("yst", (4, 5, 6, 7))
    dense("ussd0", 0)
    dense("ussd1", 1)
    norm(1)
    dense("wo0", 0)
    dense("wo1", 1)
    dense("mk0", 0)
    dense("mk1", 1)
    dense("mv0", 0)
    norm(2)
    dense("mv1", 1)
    dense("xq0", 0)
    dense("xq1", 1)
    banks("xs", (4, 5, 6, 7))
    banks("xp", (0, 1, 2, 3))
    banks("xov", (4, 5, 6, 7))
    dense("xo0", 0)
    dense("xo1", 1)
    norm(3)
    ffn(0)
    norm(4)
    ffn(1)
    norm(5)
    dense("mdown", 0, Q_LORA + KV_LORA + ROPE)
    banks("cqt", (4, 5))
    for gi in range(2):
        g = group(f"uq{gi}", 2 * 768)
        bank(("qr", gi), 2 + gi)
        bank(("qn", 2 * gi), 4 + 2 * gi)
        bank(("qn", 2 * gi + 1), 5 + 2 * gi)
        free_by_bank(g, 5 + 2 * gi)
    g = group("ukv", GROUP)
    for h2 in range(4):
        bank(("kn", h2), 4 + h2)
    banks("kvv", (0, 1, 2, 3))
    free_by_bank(g, 3)
    banks("qrt", (0, 1))
    banks("krt", (2,))
    attention(0, bank)
    dense("mo0", 0)
    dense("mo1", 1)
    norm(6)
    ffn(2)
    ple(0, banks, group, free_by_bank, norm, dense, 7)
    norm(8)
    ffn(3)
    norm(9)
    dense("fq0", 0)
    banks("small1", (3,))
    banks("row", (2,))
    dense("fq1", 1)
    for c in range(2):
        dense(f"fk{c}", c)
    attention(1, bank, dense)
    dense("fo0", 0)
    dense("fo1", 1)
    norm(10)
    ffn(4)
    ple(1, banks, group, free_by_bank, norm, dense, 11)
    return use, first, freed, cols


def attention(a, bank, dense=None):
    for h in range(4):
        bank((f"as{a}", h), 4 + h)
    if dense:
        dense("fv0", 1)
    for h in range(8):
        bank((f"ap{a}", h), h % 2)
        if h + 4 < 8:
            bank((f"as{a}", h + 4), 4 + h)
        bank((f"ao{a}", h), 2 + h % 2)
        if dense and h == 3:
            dense("fv1", 0)


def ple(l, banks, group, free_by_bank, norm, dense, n):
    banks(f"pt{l}", (3,))
    g = group(f"pp{l}", GROUP)
    banks(f"pp{l}", (0, 1, 2, 3))
    free_by_bank(g, 3)
    norm(n)
    dense(f"pg{l}0", 2)
    dense(f"pg{l}1", 3)


def build(nc, A, out):
    use, first, freed, cols = lay_out()
    n_groups = len(freed)

    with ExitStack() as ctx:
        def sb(name, shape, dt=F32):
            return ctx.enter_context(nc.sbuf_tensor(name, shape, dt))

        def sem(name):
            return ctx.enter_context(nc.semaphore(name))

        w_raw = sb("w_raw", [P, RING, GROUP])
        w_hi = sb("w_hi", [P, RING, GROUP], F32R)
        w_lo = sb("w_lo", [P, RING, GROUP], F32R)
        t1h, t1l = sb("t1h", [P, KD, S], F32R), sb("t1l", [P, KD, S], F32R)
        t2h, t2l = sb("t2h", [P, KD, S], F32R), sb("t2l", [P, KD, S], F32R)
        h = sb("h", [P, NT, D])
        tma, tmb, tmc, tmd, tme = (sb(f"tm{x}", [P, NT, D]) for x in "abcde")
        fma, fmb = sb("fma", [P, KD, S]), sb("fmb", [P, KD, S])
        fms = sb("fms", [P, 4, S])
        fmt = sb("fmt", [P, 4, S])
        pair = sb("pair", [P, 4, 384])
        k2 = sb("k2", [P, 4, P])
        q3 = sb("q3", [P, 4, CHUNK])
        cbt = sb("cbt", [P, 2, 384])
        tab = sb("tab", [P, T_END])
        col = sb("col", [P, C_END])
        bcast = sb("bcast", [P, 56])
        ws_raw = sb("ws_raw", [P, KD, 32])
        ws_hi, ws_lo = sb("ws_hi", [P, KD, 32], F32R), sb("ws_lo", [P, KD, 32], F32R)
        wa2 = sb("wa2", [GLA_RANK, 512])
        a1t = sb("a1t_sb", [GLA_RANK, S])
        ss, var, rstd, power = sb("ss", [P, 8]), sb("var", [P, 8]), sb("rstd", [P, 8]), sb("power", [P, 8])
        sm = sb("sm", [P, 4, 16])
        dtw = sb("dtw", [P, 8, NT, 16])
        dt = sb("dt", [P, NT, 16])
        da = sb("da", [P, NT, 16])
        ga = sb("ga", [P, NT, 16])
        pos_i, pos_f = sb("pos_i", [P, NT], I32), sb("pos_f", [P, NT])
        rot = sb("rot", [P, 2, NT, ROPE])
        decay = sb("decay", [P, 8])
        scales = sb("scales", [P, 8])
        ps = [ctx.enter_context(nc.psum_tensor(f"bank{b}", [P, 512], F32)) for b in range(8)]

        ident = tab[:, T_ID:T_ID + P]
        tri1 = tab[:, T_TRI:T_TRI + 2 * P]
        ones_upper = tab[:, T_OU:T_OU + 2 * P]

        w_loaded = [sem(f"w_loaded{i}") for i in range(RING)]
        w_hi_ready, w_lo_ready, w_used = sem("w_hi_ready"), sem("w_lo_ready"), sem("w_used")
        bank_full = [sem(f"bank_full{b}") for b in range(8)]
        bank_free = [sem(f"bank_free{b}") for b in range(8)]
        x_loaded, tab_loaded, rows_loaded, small_loaded = (sem(x) for x in ("x_loaded", "tab_loaded", "rows_loaded", "small_loaded"))
        ident_loaded, row_mix_loaded, rest_loaded = (sem(x) for x in ("ident_loaded", "row_mix_loaded", "rest_loaded"))
        mem_loaded, row_loaded, p_loaded, fox_loaded = (sem(x) for x in ("mem_loaded", "row_loaded", "p_loaded", "fox_loaded"))
        out_stored = sem("out_stored")
        sq_done, var_ready, rstd_ready, xn_ready = (sem(x) for x in ("sq_done", "var_ready", "rstd_ready", "xn_ready"))
        operand_hi = sem("operand_hi")
        act_step, dve_step, pool_step = sem("act_step"), sem("dve_step"), sem("pool_step")
        events = {}

        def event(name):
            if name not in events:
                events[name] = sem(name)
            return events[name]

        w_in_v = A["w_in"].rearrange("a (k p) n -> p (a k) n", p=P)

        def square(name, l=0):
            return A[name].rearrange("a (k p) n -> a p k n", p=P)[l]

        ffn_in = [A["w_ffn_in"].rearrange("a (k p) (t n) -> a p k t n", p=P, t=2)[0]] + [
            A["ffn_w_in_2"].rearrange("a b (k p) (t n) -> a b p k t n", p=P, t=2)[l, m] for l in range(2) for m in range(2)]
        ffn_out = [A["w_ffn_out"].rearrange("a (k p) n -> a p k n", p=P)[0]] + [
            A["ffn_w_out_2"].rearrange("a b (k p) n -> a b p k n", p=P)[l, m] for l in range(2) for m in range(2)]

        dense_src = {}
        for key, c0, n in (("xbc", XBC0, 3), ("q", Q0, 0), ("k", K0, 0), ("v", V0, 2), ("r", R0, 2), ("z", Z0, 2),
                           ("gs", GS0, 2), ("gg", GG0, 2)):
            for c in range(max(n, 1)):
                dense_src[f"{key}{c}" if n else key] = (w_in_v, c0 + 512 * c, 512)
        for key, name, l, c0 in (("ugla", "w_up_gla", 0, 0), ("ussd", "w_up_ssd", 0, 0), ("wo", "w_o", 0, 0),
                                 ("mk", "w_xkv", 0, 0), ("mv", "w_xkv", 0, D), ("xq", "w_xq", 0, 0), ("xo", "w_xo", 0, 0),
                                 ("mo", "mla_w_o_2", 0, 0), ("fq", "fox_w_in_2", 0, 0), ("fk", "fox_w_in_2", 0, D),
                                 ("fv", "fox_w_in_2", 0, 2 * D), ("fo", "fox_w_o_2", 0, 0),
                                 ("pg0", "ple_w_gate_2", 0, 0), ("pg1", "ple_w_gate_2", 1, 0)):
            for c in range(2):
                dense_src[f"{key}{c}"] = (square(name, l), c0 + 512 * c, 512)
        dense_src["mdown"] = (square("mla_w_down_2"), 0, Q_LORA + KV_LORA + ROPE)

        def raw(g, k, *shape):
            n = cols[g] if isinstance(g, int) else GROUP
            return w_raw[:, g % RING, 0:n].rearrange("p (k n) -> p k n", k=k)

        sources = {}
        for name, (w, c0, width) in dense_src.items():
            g = first[name]
            for half in range(2):
                sources[g + half] = (4, w[:, 4 * half:4 * half + 4, c0:c0 + width])
        for gi in range(2):
            sources[first[f"uq{gi}"]] = (2, square("mla_w_uq_2")[:, :, 768 * gi:768 * gi + 768])
        sources[first["ukv"]] = (1, square("mla_w_ukv_2"))
        for l in range(2):
            sources[first[f"pp{l}"]] = (2, square("ple_w_proj_2", l))
        for n in range(N_FFN):
            g0 = first[f"ffn{n}"]
            for half in range(2):
                sources[g0 + half] = ("gu", n, half, 0)
            sources[g0 + 3 * NJ - 1] = (2, ffn_out[n][:, 2 * (NJ - 1):2 * NJ, :])

        def full(e, key):
            b, i = use[key]
            e.wait_ge(bank_full[b], i + 1)
            return ps[b]

        def drained(e, *keys):
            for key in keys:
                b, i = use[key]
                e.wait_ge(bank_free[b], i + 1)

        def free(ins, key):
            ins.then_inc(bank_free[use[key][0]], 1)

        def quad(name):
            return [(name, q) for q in range(4)]

        x_fm, x_tok, silu_z, silu_r = fma, tma, tmb, tmd
        v_tok = tmc
        gate_s = fma
        gate_g = tmd.rearrange("p t (k s) -> p (t k) s", s=S)
        q_fm, k_fm = fmb[:, 0:4, :], fmb[:, 4:8, :]
        gla_bs = tme[:, 0, :].rearrange("p (a s) -> p a s", a=4)
        gla_eb = tme[:, 1, :].rearrange("p (a s) -> p a s", a=4)
        gla_nv = tmb[:, 0, :].rearrange("p (a s) -> p a s", a=4)
        gla_av = tmb[:, 1, :].rearrange("p (a s) -> p a s", a=4)
        kt, kh = fms, fmt
        silu_g = tme[:, 0, 0:2 * FB].rearrange("p (t f) -> p t f", t=NT)
        ffn_h = tme[:, 0, 2 * FB:4 * FB].rearrange("p (t f) -> p t f", t=NT)
        upper = ones_upper[:, P:2 * P]
        k_rope = q3.rearrange("p a c -> p (a c)")
        diag, row = tme[:, 0, 0:S], tme[:, 0, S:2 * S]
        rows_a, rows_b, rows_c = (tmd[:, 0, P * i:P * i + P] for i in range(3))
        rows_of = lambda ap: ap.rearrange("a (k p) -> (a k) p", p=P)
        norm_rows = [rows_of(A["norm_mem"]), rows_of(A["norm_xattn"]), rows_of(A["norm_ffn"]),
                     A["ffn_norm_2"].rearrange("a b (k p) -> (a b k) p", p=P), rows_of(A["mix_norm_2"]), rows_of(A["ple_norm_2"]),
                     A["norm_final"].rearrange("(k p) -> k p", p=P)]
        other_rows = [A["ssd_conv_w"].rearrange("a i b (k p) -> (a i b k) p", p=P), rows_of(A["ssd_conv_b"]), rows_of(A["gla_b_a"]),
                      rows_of(A["mla_q_norm_2"]), rows_of(A["mla_kv_norm_2"]), rows_of(A["ssd_norm"]), rows_of(A["gla_norm"])]
        n_rows_b = C_END - C_CONVW

        def steps_mat(i):
            region = (fms if i % 4 < 2 else fmt).rearrange("p a s -> p (a s)")
            return region[:, 384 * (i % 2):384 * (i % 2) + 384]

        def probs_turned(i):
            return tmd.rearrange("p t n -> p (t n)")[:, 384 * (i % 4):384 * (i % 4) + 384]

        def outputs_after(a, i):
            if i == 7:
                return (6, 7)
            if a == 1 and i in (3, 4):
                return (2, 3) if i == 3 else ()
            return (i - 1,) if i else ()

        def cols_of(i, n=1):
            return col[:, i:i + n]

        STATS = ["norm0", "gla", "ssd", "norm1", "norm2", "norm3", "final0", "norm4", "norm5", "mla", "norm6", "norm7",
                 "norm8", "norm9", "norm10", "norm11", "final1"]
        T1, T2 = (t1h, t1l), (t2h, t2l)
        T_OF_NORM = [T2 if n == 2 or n >= 8 else T1 for n in range(12)]
        T_OF_HIDDEN = [T2, T2, T2, T1, T1]
        NORM_OF_FFN = [3, 4, 6, 8, 10]
        NORM_AFTER_FFN = [4, 5, 7, 9, 11]
        PLE_OF_FFN = {2: 0, 4: 1}
        STAT_COLS = {"gla": (0, 8), "ssd": (0, 4), "final0": (2, 4), "mla": (4, 8)}
        GAINS = [[C_NORM + 8 * GAIN_AT[n] + k for k in range(KD)] for n in range(12)]
        GAINS[4] = [C_FINAL + k for k in range(KD)]

        def h_ready(e, stage):
            if stage == "x":
                e.wait_ge(x_loaded, 32)
            elif stage == "mem":
                e.wait_ge(mem_loaded, 32)
            elif stage in ("wo", "xo", "mo", "fo"):
                drained(e, *((f"{stage}{c}", t) for c in range(2) for t in range(NT)))
            elif stage[:3] == "acc":
                drained(e, *quad(stage))
            elif stage == "gained":
                e.wait_ge(event("h_gained"), 1)
            else:
                e.wait_ge(event("h_embedded"), 4 * (int(stage[-1]) + 1))

        def h_half_ready(e, stage, c):
            if stage[:3] == "acc":
                drained(e, (stage, 2 * c), (stage, 2 * c + 1))
            elif stage[:3] == "ple":
                e.wait_ge(event("h_embedded"), 4 * int(stage[-1]) + 2 * (c + 1))
            else:
                drained(e, (f"{stage}{c}", 0), (f"{stage}{c}", 1))

        UPDATE_BEFORE = {3: "xo", 4: "acc0", 5: "acc1", 6: "mo", 7: "acc2", 8: "ple0", 9: "acc3", 10: "fo", 11: "acc4"}
        NORM_AFTER = ["x", "mem", "wo", "xo", "final0", "acc1", "mo", "acc2", "ple0", "acc3", "fo", "acc4"]
        NORM_SRC = [tmb if n == 1 else h for n in range(12)]

        block = ctx.enter_context(nc.Block())

        @block.sync
        def _(sp):
            sp.dma_start(h[:, 0, :], A["x"][0, 0:P, :]).then_inc(x_loaded, 16)
            sp.dma_start(h[:, 1, :], A["x"][0, P:S, :]).then_inc(x_loaded, 16)

            def gate_up_src(n, half, j):
                return ffn_in[n][:, 4 * half:4 * half + 4, :, bass.ts(j, FB)]

            def gate_up_dst(slot):
                return w_raw[:, slot, :].rearrange("p (k t n) -> p k t n", k=4, t=2)

            def load(g):
                if g >= RING:
                    sp.wait_ge(w_lo_ready, g - RING + 1)
                if sources[g][0] == "gu":
                    _, n, half, j = sources[g]
                    for t in range(2):
                        ins = sp.dma_start(gate_up_dst(g % RING)[:, :, t, :], gate_up_src(n, half, j)[:, :, t, :])
                        ins.then_inc(w_loaded[g % RING], 16)
                else:
                    k, src = sources[g]
                    half_p = P // 2
                    for t in range(2):
                        part = slice(t * half_p, (t + 1) * half_p)
                        sp.dma_start(raw(g, k)[part], src[part]).then_inc(w_loaded[g % RING], 16)

            def parameters():
                for dst, aps in ((rows_b, other_rows), (rows_a, norm_rows)):
                    at = 0
                    for ap in aps:
                        n = ap.shape[0]
                        sp.dma_start(dst[at:at + n, :], ap).then_inc(rows_loaded, 16)
                        at += n
                sp.dma_start(wa2[:, :], A["gla_w_a2"][0]).then_inc(rest_loaded, 16)
                for i, name in enumerate(("ssd_dt_bias", "ssd_A_log", "ssd_D")):
                    sp.dma_start(bcast[:, 16 * i:16 * i + 16], A[name][0].partition_broadcast(P)).then_inc(rest_loaded, 16)
                sp.dma_start(bcast[:, 48:56], A["fox_b_f_2"][0].partition_broadcast(P)).then_inc(rest_loaded, 16)
                sp.dma_start(pos_i[:, :], A["positions_2"].rearrange("a (t p) -> p (a t)", p=P),
                               allow_slow_non_contiguous=True).then_inc(rest_loaded, 16)
                sp.dma_start(tab[:, T_TRI:T_END], A["tables"][:, T_TRI:T_END]).then_inc(tab_loaded, 16)

            g = 0
            while g < n_groups:
                n = next((n for n in range(N_FFN) if first[f"ffn{n}"] == g), None)
                if n is None:
                    load(g)
                    g += 1
                    if g == RING:
                        parameters()
                    continue
                load(g)
                load(g + 1)
                with sp.Fori(1, NJ) as i:
                    for r in range(3):
                        c = g - 1 + r
                        slot = c % RING
                        if r < 2:
                            pieces = [(gate_up_dst(slot)[:, :, t, :], gate_up_src(n, r, i)[:, :, t, :]) for t in range(2)]
                        else:
                            down = ffn_out[n].rearrange("p (j k) n -> p j k n", k=2)[:, bass.ds(i - 1, 1), :, :]
                            dst = w_raw[:, slot, :].rearrange("p (j k n) -> p j k n", j=1, k=2)
                            pieces = [(dst[:, :, t:t + 1, :], down[:, :, t:t + 1, :]) for t in range(2)]
                        sp.wait_ge(w_lo_ready, 3 * i + (c - RING + 1))
                        for d, s in pieces:
                            sp.dma_start(d, s).then_inc(w_loaded[slot], 16)
                g += 3 * NJ
                load(g - 1)
            sp.wait_ge(event("y_out"), 2)
            sp.dma_start(out[0, 0:P, :], tmb[:, 0, :]).then_inc(out_stored, 16)
            sp.dma_start(out[0, P:S, :], tmb[:, 1, :]).then_inc(out_stored, 16)
            sp.wait_ge(out_stored, 32)

        @block.scalar
        def _(act):
            stepped = [0]

            def step(ins):
                ins.then_inc(act_step, 1)
                stepped[0] += 1

            def hi(g):
                if g >= n_groups:
                    return
                if g >= RING:
                    why = freed[g - RING]
                    if why[0] == "used":
                        act.wait_ge(w_used, why[1])
                    else:
                        act.wait_ge(bank_full[why[1]], why[2])
                act.wait_ge(w_loaded[g % RING], 32 * (g // RING + 1))
                n = cols[g]
                nc.scalar.activation(w_hi[:, g % RING, 0:n], w_raw[:, g % RING, 0:n], ACT.Copy).then_inc(w_hi_ready, 1)

            def squares(key, src, t_after):
                h_ready(act, t_after)
                c = STAT_COLS.get(key, (0, 2))[0]
                nc.scalar.activation(tme[:, 0, :], src[:, 0, :], ACT.Square, accum_out=ss[:, c:c + 1]).then_inc(sq_done, 1)

            def norm_begin(n):
                squares(f"norm{n}", NORM_SRC[n], NORM_AFTER[n])
                act.wait_ge(rstd_ready, STATS.index(f"norm{n}") + 1)
                nc.scalar.activation(tme[:, 1, :], NORM_SRC[n][:, 1, :], ACT.Copy, scale=rstd[:, 1:2]).then_inc(xn_ready, 1)

            def operand(bank_key, dst, gains=None):
                b = full(act, bank_key)
                k = dst.shape[1]
                if gains is None:
                    nc.scalar.activation(dst, b[:, 0:k * S].rearrange("p (k s) -> p k s", k=k), ACT.Copy).then_inc(operand_hi, 1)
                    return
                for i in range(k):
                    ins = nc.scalar.activation(dst[:, i, :], b[:, i * S:(i + 1) * S], ACT.Copy, scale=cols_of(gains[i]))
                ins.then_inc(operand_hi, 1)

            def norm_parts(n, qs):
                for q in qs:
                    operand((f"norm{n}", q), T_OF_NORM[n][0][:, 2 * q:2 * q + 2, :], GAINS[n][2 * q:2 * q + 2])

            def norm_end(n):
                norm_parts(n, range(4))

            def after_update(n, weights):
                weights()
                if n == 4:
                    squares("final0", h, "acc0")
                else:
                    squares(f"norm{n}", h, UPDATE_BEFORE[n])
                norm_parts(n, (2, 3))

            def rstd_of(n):
                act.wait_ge(rstd_ready, STATS.index(f"norm{n}") + 1)

            def dense_before_norm(name, n, evacuate=None):
                hi(first[name] + RING)
                norm_parts(n, (0, 1))
                if evacuate is not None:
                    for t in range(2):
                        evacuate(t, (name, t))
                after_update(n, lambda: hi(first[name] + RING + 1))

            def dense(name, evacuate=None):
                hi(first[name] + RING)
                if evacuate is not None:
                    for t in range(2):
                        evacuate(t, (name, t))
                hi(first[name] + RING + 1)

            def ffn(n):
                g0, u0 = first[f"ffn{n}"], first[f"ffn{n}_used"]
                b0, b1, b2 = (use[k][1] for k in ((f"gu{n}", 0), (f"gu{n}", 1), (f"ht{n}", 0)))

                def in_loop_hi(r, i):
                    c = g0 - 1 + r + RING
                    if r == 1:
                        act.wait_ge(bank_full[1], i + (b1 + 1))
                    else:
                        act.wait_ge(w_used, 2 * i + (u0 + (r > 0)))
                    act.wait_ge(w_loaded[c % RING], 32 * i + 32 * (c // RING + 1))
                    nc.scalar.activation(w_hi[:, c % RING, :], w_raw[:, c % RING, :], ACT.Copy).then_inc(w_hi_ready, 1)

                scale = scales[:, 0:2] if n == 1 else rstd[:, 0:2]

                def silu(j):
                    for t, b in ((0, b0), (1, b1)):
                        act.wait_ge(bank_full[t], j + (b + 1))
                        nc.scalar.activation(silu_g[:, t, :], ps[t][:, 0:FB], ACT.Silu, scale=scale[:, t:t + 1]).then_inc(event("gate_ready"), 1)

                def turned(j, k=0):
                    act.wait_ge(bank_full[2], j + (b2 + 1))
                    dst = T_OF_HIDDEN[n][0][:, k:k + 2, :].rearrange("p k s -> p (k s)")
                    nc.scalar.activation(dst, ps[2][:, :], ACT.Copy).then_inc(operand_hi, 1)

                hi(g0 + RING)
                if n == 1:
                    squares("norm4", h, "gained")
                    act.wait_ge(event("scale_ready"), 1)
                else:
                    rstd_of(NORM_OF_FFN[n])
                silu(0)
                hi(g0 + RING + 1)
                turned(0)
                if n in PLE_OF_FFN:
                    operand((f"pt{PLE_OF_FFN[n]}", 0), T_OF_HIDDEN[n][0][:, 2:4, :])

                with act.Fori(1, NJ - 1) as i:
                    in_loop_hi(0, i)
                    silu(i)
                    in_loop_hi(1, i)
                    turned(i)
                    in_loop_hi(2, i)
                in_loop_hi(0, NJ - 1)
                silu(NJ - 1)
                turned(NJ - 1, 4)
                in_loop_hi(1, NJ - 1)
                in_loop_hi(2, NJ - 1)
                norm_parts(NORM_AFTER_FFN[n], (0, 1))
                after_update(NORM_AFTER_FFN[n], lambda: hi(g0 + 3 * NJ - 1 + RING))

            act.dma_start(rows_c[0:KD, :], rows_of(A["norm_mix"])).then_inc(row_mix_loaded, 16)
            act.dma_start(tab[:, T_ID:T_ID + P], A["tables"][:, T_ID:T_ID + P]).then_inc(ident_loaded, 16)
            act.dma_start(ws_raw[:, :, 0:16], w_in_v[:, :, DT0:DT0 + 16]).then_inc(small_loaded, 16)
            act.dma_start(ws_raw[:, :, 16:32], w_in_v[:, :, A10:A10 + 16]).then_inc(small_loaded, 16)

            norm_begin(0)
            hi(0)
            hi(1)
            hi(2)
            act.wait_ge(small_loaded, 16 * 2)
            nc.scalar.activation(ws_hi[:, :, :], ws_raw[:, :, :], ACT.Copy).then_inc(event("small_hi"), 1)
            drained(act, ("cols", 0))
            norm_end(0)
            drained(act, ("cols", 1), ("cols", 2))

            def conv(c, dst):
                def first_tap(b, key):
                    bank = full(act, key)
                    for f in range(2):
                        j = 4 * c + 2 * b + f
                        ins = nc.scalar.activation(dst[:, 2 * b + f, :], bank[:, f * S:(f + 1) * S], ACT.Identity,
                                                   bias=cols_of(C_CONVB + j), scale=cols_of(C_CONVW + 36 + j))
                    ins.then_inc(event("conv_first"), 1)
                dense(f"xbc{c}", first_tap)

            def conv_silu(c, dst):
                drained(act, (f"xbc{c}", 0), (f"xbc{c}", 1))
                nc.scalar.activation(dst, dst, ACT.Silu).then_inc(event("conv_done"), 1)

            parts = [x_fm[:, 0:4, :], x_fm[:, 4:8, :], fms[:, :, :]]
            conv(0, parts[0])
            conv(1, parts[1])
            conv_silu(0, parts[0])
            conv(2, parts[2])
            conv_silu(1, parts[1])

            act.wait_ge(event("gla_abs"), 1)
            step(nc.scalar.activation(gla_av, gla_av, ACT.Exp, scale=-1.0))
            act.wait_ge(act_step, stepped[0])
            nc.scalar.activation(gla_av, gla_av, ACT.Ln, bias=1.0).then_inc(event("gla_log"), 1)

            def q_part(b, key):
                bank = full(act, key)
                free(nc.scalar.activation(q_fm[:, 2 * b:2 * b + 2, :], bank[:, :].rearrange("p (k s) -> p k s", k=2), ACT.Copy,
                                          scale=GLA_DK ** -0.5), key)
            dense("q", q_part)
            conv_silu(2, parts[2])

            def k_part(b, key):
                bank = full(act, key)
                free(nc.scalar.activation(k_fm[:, 2 * b:2 * b + 2, :], bank[:, :].rearrange("p (k s) -> p k s", k=2), ACT.Copy), key)
            dense("k", k_part)

            act.wait_ge(event("angles"), 1)
            nc.scalar.activation(rot[:, 1, :, 32:64], rot[:, 0, :, 0:32], ACT.Sin).then_inc(event("sines"), 1)
            nc.scalar.activation(rot[:, 1, :, 0:32], rot[:, 0, :, 0:32], ACT.Sin, scale=0.5).then_inc(event("sines"), 1)

            act.wait_ge(event("dt_abs"), 1)
            act.wait_ge(rest_loaded, 16 * 6)
            step(nc.scalar.activation(dtw[:, 1, :, :], dtw[:, 1, :, :], ACT.Exp, scale=-1.0))
            act.wait_ge(act_step, stepped[0])
            step(nc.scalar.activation(dtw[:, 2, :, :], dtw[:, 1, :, :], ACT.Ln, bias=1.0))
            nc.scalar.activation(dtw[:, 7, 0, :], bcast[:, 16:32], ACT.Exp).then_inc(event("dt_log"), 1)

            def v_part(c, scaled=False):
                def part(t, key):
                    bank = full(act, key)
                    free(nc.scalar.activation(v_tok[:, t, 512 * c:512 * c + 512], bank[:, :], ACT.Copy,
                                              scale=rstd[:, t:t + 1] if scaled else 1.0), key)
                return part

            def silu_part(dst, c):
                def part(t, key):
                    bank = full(act, key)
                    free(nc.scalar.activation(dst[:, t, 512 * c:512 * c + 512], bank[:, :], ACT.Silu), key)
                return part

            act.wait_ge(event("gla_sums"), 1)
            nc.scalar.activation(gla_eb, gla_bs, ACT.Exp, scale=-1.0 / GLA_TAU).then_inc(event("gla_exp"), 1)
            full(act, ("cbt", 1))
            nc.scalar.activation(kt[:, :, :], gla_bs, ACT.Exp, scale=1.0 / GLA_TAU).then_inc(event("gla_exp"), 1)
            nc.scalar.activation(kh[:, :, :], gla_av, ACT.Exp, scale=1.0 / GLA_TAU).then_inc(event("gla_exp"), 1)
            dense("v0", v_part(0))
            for q in range(4):
                bank = full(act, ("xt", q))
                free(nc.scalar.activation(x_tok[:, q // 2, 512 * (q % 2):512 * (q % 2) + 512], bank[:, :], ACT.Copy), ("xt", q))
            dense("v1", v_part(1))
            dense("r0", silu_part(silu_r, 0))
            dense("r1", silu_part(silu_r, 1))
            dense("z0", silu_part(silu_z, 0))

            for q in range(4):
                bank = full(act, ("glao", q))
                for i in range(2):
                    at = 512 * (q % 2) + GLA_DV * i
                    ins = nc.scalar.activation(tme[:, q // 2, at:at + GLA_DV], bank[:, GLA_DV * i:GLA_DV * (i + 1)], ACT.Square,
                                               accum_out=ss[:, 2 * q + i:2 * q + i + 1])
            ins.then_inc(sq_done, 1)
            dense("z1", silu_part(silu_z, 1))

            def tanh_part(dst, c):
                def part(b, key):
                    bank = full(act, key)
                    free(nc.scalar.activation(dst[:, 4 * c + 2 * b:4 * c + 2 * b + 2, :], bank[:, :].rearrange("p (k s) -> p k s", k=2),
                                              ACT.Tanh, scale=0.5), key)
                return part

            for hg in range(4):
                for i in range(4 * hg, 4 * hg + 4):
                    bank = full(act, ("ssd_d", i))
                    nc.scalar.activation(bank[:, 0:384], bank[:, 0:384], ACT.Exp).then_inc(event("ssd_exp"), 1)
                if hg in (1, 2):
                    for q in (2 * hg - 2, 2 * hg - 1):
                        operand(("ygt", q), t2h[:, 2 * q:2 * q + 2, :], [C_GLAN, C_GLAN + 1])
                dense(("gs0", "gs1", "gg0", "gg1")[hg], tanh_part(gate_s if hg < 2 else gate_g, hg % 2))
            drained(act, ("ssd_y", 3))
            act.wait_ge(event("y_gated"), 4)
            for i in range(4):
                t, g = i // 2, i % 2
                ins = nc.scalar.activation(tme[:, t, 512 * g:512 * g + 512], tmc[:, t, 512 * g:512 * g + 512], ACT.Square, accum_out=ss[:, i:i + 1])
            ins.then_inc(sq_done, 1)
            for t in range(NT):
                act.dma_start(tmb[:, t, :], A["mem"][0, t * P:(t + 1) * P, :]).then_inc(mem_loaded, 16)
            act.dma_start(tma[:, 0, :], A["norm_final"].partition_broadcast(P)).then_inc(row_loaded, 16)
            act.dma_start(tma[:, 1, :], A["final_norm_2"].partition_broadcast(P)).then_inc(row_loaded, 16)
            dense("ugla0")
            for q in range(4):
                operand(("yst", q), t1h[:, 2 * q:2 * q + 2, :], [C_SSDN + 2 * q, C_SSDN + 2 * q + 1])
            dense("ugla1")

            norm_begin(1)
            for c in range(2):
                hi(first[f"ussd{c}"] + RING)
                for b in range(2):
                    k = 4 * c + 2 * b
                    act.wait_ge(event("merged"), 2 * c + b + 1)
                    nc.scalar.activation(t2h[:, k:k + 2, :], gate_s[:, k:k + 2, :], ACT.Copy, scale=0.5).then_inc(operand_hi, 1)
                hi(first[f"ussd{c}"] + RING + 1)
            norm_end(1)
            dense("wo0")
            dense("wo1")

            def fm_part(dst, c, scale=1.0):
                def part(b, key):
                    bank = full(act, key)
                    free(nc.scalar.activation(dst[:, 4 * c + 2 * b:4 * c + 2 * b + 2, :], bank[:, :].rearrange("p (k s) -> p k s", k=2),
                                              ACT.Copy, scale=scale), key)
                return part

            norm_begin(2)
            dense("mk0", fm_part(fmb, 0))
            dense("mk1", fm_part(fmb, 1))
            dense("mv0", v_part(0))
            norm_end(2)
            dense("mv1", v_part(1))
            dense("xq0", fm_part(fma, 0))
            dense("xq1", fm_part(fma, 1))

            for i in range(X_HEADS):
                act.wait_ge(event("soft_max"), i + 1)
                bank = full(act, ("xs", i))
                for t in range(NT):
                    at = 2 * i + t
                    ins = nc.scalar.activation(tmb[:, t, S * i:S * i + S], bank[:, S * t:S * t + S], ACT.Exp, bias=sm[:, 1, at:at + 1],
                                               scale=X_DH ** -0.5, accum_out=sm[:, 2, at:at + 1])
                free(ins, ("xs", i))
            for i in range(X_HEADS):
                bank = full(act, ("xp", i))
                free(nc.scalar.activation(tmd[:, i // 2, 512 * (i % 2):512 * (i % 2) + 512], bank[:, :], ACT.Copy), ("xp", i))
            for i in range(X_HEADS):
                operand(("xov", i), t2h[:, 2 * i:2 * i + 2, :])
            dense("xo0")
            dense_before_norm("xo1", 3)
            ffn(0)
            act.dma_start(fmt[:, 0:2, :], A["p_2"][0, 0].rearrange("(t p) n -> p t n", p=P)).then_inc(p_loaded, 16)
            act.dma_start(ws_raw[:, :, 0:FOX_HEADS], square("fox_w_in_2")[:, :, 3 * D:3 * D + FOX_HEADS]).then_inc(fox_loaded, 16)
            ffn(1)

            hi(first["mdown"] + RING)
            rstd_of(5)
            for t in range(NT):
                bank = full(act, ("mdown", t))
                nc.scalar.activation(tme[:, t, 0:Q_LORA], bank[:, 0:Q_LORA], ACT.Square, scale=rstd[:, t:t + 1], accum_out=ss[:, 4 + t:5 + t])
                ins = nc.scalar.activation(tme[:, t, Q_LORA:Q_LORA + KV_LORA], bank[:, Q_LORA:Q_LORA + KV_LORA], ACT.Square,
                                           scale=rstd[:, t:t + 1], accum_out=ss[:, 6 + t:7 + t])
            ins.then_inc(sq_done, 1)
            hi(first["mdown"] + RING + 1)
            operand(("cqt", 0), t2h[:, 0:2, :], [C_QN, C_QN + 1])
            operand(("cqt", 1), t2h[:, 2:3, :], [C_KVN])
            scale = (NOPE + ROPE) ** -0.5
            for gi in range(2):
                hi(first[f"uq{gi}"] + RING)
                for q in range(2 * gi, 2 * gi + 2):
                    bank = full(act, ("qn", q))
                    free(nc.scalar.activation(fma[:, 2 * q:2 * q + 2, :], bank[:, :].rearrange("p (k s) -> p k s", k=2), ACT.Copy,
                                              scale=scale), ("qn", q))
            for q in range(4):
                bank = full(act, ("kn", q))
                free(nc.scalar.activation(fmb[:, 2 * q:2 * q + 2, :], bank[:, :].rearrange("p (k s) -> p k s", k=2), ACT.Copy), ("kn", q))
            for q in range(4):
                bank = full(act, ("kvv", q))
                free(nc.scalar.activation(tmc[:, q // 2, 512 * (q % 2):512 * (q % 2) + 512], bank[:, :], ACT.Copy), ("kvv", q))
            hi(first["ukv"] + RING)
            for q in range(2):
                bank = full(act, ("qrt", q))
                free(nc.scalar.activation(fms[:, 2 * q:2 * q + 2, :], bank[:, :].rearrange("p (k s) -> p k s", k=2), ACT.Copy,
                                          scale=scale), ("qrt", q))
            bank = full(act, ("krt", 0))
            free(nc.scalar.activation(k_rope, bank[:, 0:S], ACT.Copy), ("krt", 0))

            def attention(a):
                def soft(i):
                    act.wait_ge(event("soft_max"), X_HEADS + 8 * a + i + 1)
                    for t, (c0, c1) in enumerate(((0, P), (P, 3 * P))):
                        at = 2 * i + t
                        ins = nc.scalar.activation(pair[:, i % 4, c0:c1], pair[:, i % 4, c0:c1], ACT.Exp, bias=sm[:, 1, at:at + 1],
                                                   accum_out=sm[:, 2, at:at + 1])
                    ins.then_inc(event("soft_exp"), 1)
                for i in range(4):
                    soft(i)
                if a == 1:
                    dense("fv0", v_part(0, True))
                th = (T2, T1)[a][0]
                for i in range(8):
                    bank = full(act, (f"ap{a}", i))
                    free(nc.scalar.activation(probs_turned(i), bank[:, 0:384], ACT.Copy), (f"ap{a}", i))
                    if i + 4 < 8:
                        soft(i + 4)
                    for j in outputs_after(a, i):
                        operand((f"ao{a}", j), th[:, j:j + 1, :])
                    if a == 1 and i == 3:
                        dense("fv1", v_part(1, True))

            attention(0)
            dense("mo0")
            dense_before_norm("mo1", 6)
            ffn(2)

            def ple(l, n, next_norm):
                hi(first[f"pp{l}"] + RING)
                rstd_of(n)

                def part(c):
                    def tanh(t, key):
                        bank = full(act, key)
                        free(nc.scalar.activation(tmd[:, t, 512 * c:512 * c + 512], bank[:, :], ACT.Tanh, scale=rstd[:, t:t + 1]), key)
                    return tanh
                dense(f"pg{l}0", part(0))
                if next_norm is None:
                    dense(f"pg{l}1", part(1))
                else:
                    dense_before_norm(f"pg{l}1", next_norm, part(1))

            ple(0, 7, 8)
            ffn(3)
            act.wait_ge(fox_loaded, 16)
            nc.scalar.activation(ws_hi[:, :, 0:FOX_HEADS], ws_raw[:, :, 0:FOX_HEADS], ACT.Copy).then_inc(event("small_hi"), 1)
            hi(first["fq0"] + RING)
            bank = full(act, ("row", 0))
            free(nc.scalar.activation(row, bank[:, 0:S], ACT.Copy), ("row", 0))
            hi(first["fq0"] + RING + 1)
            act.wait_ge(event("fox_abs"), 1)
            step(nc.scalar.activation(dtw[:, 1, :, 0:8], dtw[:, 1, :, 0:8], ACT.Exp, scale=-1.0))
            act.wait_ge(act_step, stepped[0])
            nc.scalar.activation(dtw[:, 2, :, 0:8], dtw[:, 1, :, 0:8], ACT.Ln, bias=1.0).then_inc(event("fox_log"), 1)
            dense("fq1")
            dense("fk0")
            dense("fk1")
            attention(1)
            dense("fo0")
            act.dma_start(fmt[:, 0:2, :], A["p_2"][1, 0].rearrange("(t p) n -> p t n", p=P)).then_inc(p_loaded, 16)
            dense_before_norm("fo1", 10)
            ffn(4)
            ple(1, 11, None)
            act.wait_ge(event("h_embedded"), 7)
            nc.scalar.activation(tme[:, 0, :], h[:, 0, :], ACT.Square, accum_out=ss[:, 0:1]).then_inc(sq_done, 1)
            act.wait_ge(rstd_ready, STATS.index("final1") + 1)
            act.wait_ge(event("y_gained"), 1)
            nc.scalar.activation(tmb[:, 0, :], tmb[:, 0, :], ACT.Copy, scale=rstd[:, 0:1]).then_inc(event("y_out"), 1)

        @block.vector
        def _(dve):
            stepped = [0]
            his = [0]
            v = nc.vector

            def step(ins):
                ins.then_inc(dve_step, 1)
                stepped[0] += 1
                return stepped[0]

            def chain(ins):
                dve.wait_ge(dve_step, step(ins))

            def lo(g):
                if g >= n_groups:
                    return
                dve.wait_ge(w_hi_ready, g + 1)
                n = cols[g]
                v.tensor_tensor(w_lo[:, g % RING, 0:n], w_raw[:, g % RING, 0:n], w_hi[:, g % RING, 0:n].bitcast(F32), ALU.subtract)\
                    .then_inc(w_lo_ready, 1)

            def dense(name, evacuate=None):
                lo(first[name] + RING)
                if evacuate is not None:
                    for t in range(2):
                        evacuate(t, (name, t))
                lo(first[name] + RING + 1)

            def mean_squares(key, src, after):
                h_ready(dve, after)
                c = STAT_COLS.get(key, (0, 2))[0] + 1
                chain(v.tensor_tensor_reduce(tme[:, 1, :], src[:, 1, :], src[:, 1, :], 1.0, 0.0, ALU.mult, ALU.add, ss[:, c:c + 1]))
                variance(key, D, 4.0 if key in ("norm7", "norm11") else 1.0)

            def variance(key, width, factor=1.0):
                dve.wait_ge(sq_done, STATS.index(key) + 1)
                a, b = STAT_COLS.get(key, (0, 2))
                v.tensor_scalar(var[:, a:b], ss[:, a:b], factor / width, factor * EPS, ALU.mult, ALU.add).then_inc(var_ready, 1)

            def rstd_of(key):
                dve.wait_ge(rstd_ready, STATS.index(key) + 1)

            def norm_begin(n):
                src = NORM_SRC[n]
                mean_squares(f"norm{n}", src, NORM_AFTER[n])
                rstd_of(f"norm{n}")
                v.tensor_scalar(tme[:, 0, :], src[:, 0, :], rstd[:, 0:1], None, ALU.mult).then_inc(xn_ready, 1)

            def operand(key, dst, first_part, gains=None):
                his[0] += 1
                dve.wait_ge(operand_hi, his[0])
                b = ps[use[key][0]]
                k = dst.shape[1]
                if gains is None:
                    free(v.tensor_tensor(dst, b[:, 0:k * S].rearrange("p (k s) -> p k s", k=k), first_part.bitcast(F32), ALU.subtract), key)
                    return
                for i in range(k):
                    ins = v.scalar_tensor_tensor(dst[:, i, :], b[:, i * S:(i + 1) * S], cols_of(gains[i]), first_part[:, i, :].bitcast(F32),
                                                 ALU.mult, ALU.subtract)
                free(ins, key)

            def norm_parts(n, qs):
                th, tl = T_OF_NORM[n]
                for q in qs:
                    operand((f"norm{n}", q), tl[:, 2 * q:2 * q + 2, :], th[:, 2 * q:2 * q + 2, :], GAINS[n][2 * q:2 * q + 2])

            def norm_end(n):
                norm_parts(n, range(4))

            def after_update(n, weights):
                if n == 4:
                    mean_squares("final0", h, "acc0")
                norm_parts(n, (2, 3))
                if n != 4:
                    mean_squares(f"norm{n}", h, UPDATE_BEFORE[n])
                weights()

            def dense_before_norm(name, n, evacuate):
                lo(first[name] + RING)
                norm_parts(n, (0, 1))
                for t in range(2):
                    evacuate(t, (name, t))
                after_update(n, lambda: lo(first[name] + RING + 1))

            def ffn(n, factor):
                g0 = first[f"ffn{n}"]
                b0, b1, b2 = (use[k][1] for k in ((f"gu{n}", 0), (f"gu{n}", 1), (f"ht{n}", 0)))
                hi0 = his[0]

                def in_loop_lo(r, i):
                    c = g0 - 1 + r + RING
                    dve.wait_ge(w_hi_ready, 3 * i + (c + 1))
                    v.tensor_tensor(w_lo[:, c % RING, :], w_raw[:, c % RING, :], w_hi[:, c % RING, :].bitcast(F32), ALU.subtract)\
                        .then_inc(w_lo_ready, 1)

                th, tl = T_OF_HIDDEN[n]
                scale = scales[:, 0:2] if n == 1 else rstd[:, 0:2]

                def gated(j):
                    for t in range(NT):
                        dve.wait_ge(event("gate_ready"), 2 * j + (2 * NJ * n + t + 1))
                        v.scalar_tensor_tensor(ffn_h[:, t, :], ps[t][:, FB:2 * FB], scale[:, t:t + 1], silu_g[:, t, :], ALU.mult, ALU.mult)\
                            .then_inc(bank_free[t], 1)

                def turned(j, hi0, k=0):
                    dve.wait_ge(operand_hi, j + (hi0 + 1))
                    v.tensor_tensor(tl[:, k:k + 2, :].rearrange("p k s -> p (k s)"), ps[2][:, :],
                                    th[:, k:k + 2, :].rearrange("p k s -> p (k s)").bitcast(F32), ALU.subtract).then_inc(bank_free[2], 1)

                if n == 1:
                    rstd_of("final0")
                    chain(v.tensor_tensor(scales[:, 2:4], rstd[:, 2:4], rstd[:, 2:4], ALU.mult))
                    dve.wait_ge(event("h_gained"), 2)
                    chain(v.tensor_tensor_reduce(tme[:, 1, :], h[:, 1, :], h[:, 1, :], 1.0, 0.0, ALU.mult, ALU.add, ss[:, 1:2]))
                    dve.wait_ge(sq_done, STATS.index("norm4") + 1)
                    chain(v.tensor_tensor(ss[:, 0:2], ss[:, 0:2], scales[:, 2:4], ALU.mult))
                    variance("norm4", D)
                    rstd_of("norm4")
                    v.tensor_tensor(scales[:, 0:2], rstd[:, 0:2], rstd[:, 2:4], ALU.mult).then_inc(event("scale_ready"), 1)
                    lo(g0 + RING)
                    dve.wait_ge(event("scale_ready"), 1)
                else:
                    lo(g0 + RING)
                    rstd_of(f"norm{NORM_OF_FFN[n]}")
                gated(0)
                lo(g0 + RING + 1)
                turned(0, hi0)
                his[0] += 1
                if n == 1:
                    for t in range(NT):
                        v.tensor_scalar(h[:, t, :], h[:, t, :], rstd[:, 2 + t:3 + t], None, ALU.mult).then_inc(event("h_normed"), 1)
                if n in PLE_OF_FFN:
                    operand((f"pt{PLE_OF_FFN[n]}", 0), tl[:, 2:4, :], th[:, 2:4, :])

                hi_loop = his[0] - 1
                with dve.Fori(1, NJ - 1) as i:
                    in_loop_lo(0, i)
                    gated(i)
                    in_loop_lo(1, i)
                    turned(i, hi_loop)
                    in_loop_lo(2, i)
                in_loop_lo(0, NJ - 1)
                gated(NJ - 1)
                turned(NJ - 1, hi_loop, 4)
                in_loop_lo(1, NJ - 1)
                his[0] += NJ - 1

                def update(q):
                    t, c = q % 2, q // 2
                    bank = full(dve, (f"acc{n}", q))
                    part = h[:, t, 512 * c:512 * c + 512]
                    free(v.scalar_tensor_tensor(part, bank[:, :], factor, part, ALU.mult, ALU.add), (f"acc{n}", q))

                if n == 1:
                    dve.wait_ge(event("h_normed"), 2)
                for q in range(3):
                    update(q)
                norm_parts(NORM_AFTER_FFN[n], (0, 1))
                update(3)
                in_loop_lo(2, NJ - 1)
                after_update(NORM_AFTER_FFN[n], lambda: lo(g0 + 3 * NJ - 1 + RING))

            def residual(name, c):
                def part(t, key):
                    bank = full(dve, key)
                    dst = h[:, t, 512 * c:512 * c + 512]
                    free(v.tensor_tensor(dst, bank[:, :], dst, ALU.add), key)
                return part

            bank = full(dve, ("cols", 0))
            free(v.tensor_copy(col[:, 0:KD], bank[:, 0:KD]), ("cols", 0))
            norm_begin(0)
            lo(0)
            lo(1)
            lo(2)
            dve.wait_ge(event("small_hi"), 1)
            v.tensor_tensor(ws_lo[:, :, :], ws_raw[:, :, :], ws_hi[:, :, :].bitcast(F32), ALU.subtract).then_inc(event("small_lo"), 1)
            norm_end(0)
            bank = full(dve, ("small0", 0))
            small = bank[:, 0:64].rearrange("p (t c) -> p t c", t=NT)
            v.tensor_copy(dtw[:, 0, :, :], small[:, :, 0:16]).then_inc(event("dt_raw"), 1)
            free(v.tensor_copy(dtw[:, 3, :, :], small[:, :, 16:32]), ("small0", 0))

            def conv(c, dst):
                lo(first[f"xbc{c}"] + RING)
                done = {}
                for b in range(2):
                    dve.wait_ge(event("conv_first"), 2 * c + b + 1)
                    for tap in (2, 1, 0):
                        shift = 3 - tap
                        for f in (2 * b, 2 * b + 1):
                            if f in done:
                                dve.wait_ge(dve_step, done[f])
                            src = ps[use[f"xbc{c}", b][0]][:, (f % 2) * S:(f % 2) * S + S - shift]
                            ins = v.scalar_tensor_tensor(dst[:, f, shift:S], src, cols_of(C_CONVW + 12 * tap + 4 * c + f), dst[:, f, shift:S],
                                                         ALU.mult, ALU.add)
                            if tap == 0 and f % 2:
                                free(ins, (f"xbc{c}", b))
                            else:
                                done[f] = step(ins)
                lo(first[f"xbc{c}"] + RING + 1)

            bank = full(dve, ("a1t", 0))
            free(v.tensor_copy(a1t[:, :], bank[0:GLA_RANK, 0:S]), ("a1t", 0))
            for i, c0, c1 in ((1, KD, C_CONVW), (2, C_CONVW, C_END)):
                bank = full(dve, ("cols", i))
                free(v.tensor_copy(col[:, c0:c1], bank[:, 0:c1 - c0]), ("cols", i))
            drained(dve, ("cols", 1), ("cols", 2))
            at = C_NORM + 8 * GAIN_AT[4]
            v.tensor_tensor(col[:, C_FINAL:C_FINAL + KD], col[:, C_FINAL:C_FINAL + KD], col[:, at:at + KD], ALU.mult)\
                .then_inc(event("gains_joined"), 1)

            conv(0, fma[:, 0:4, :])
            conv(1, fma[:, 4:8, :])
            for i in range(GLA_HEADS):
                bank = full(dve, ("la", i // 2))
                ins = v.tensor_scalar(gla_nv[:, i, :], bank[:, (i % 2) * S:(i % 2) * S + S], -1.0, cols_of(C_BA + i), ALU.mult, ALU.subtract)
                if i % 2:
                    free(ins, ("la", i // 2))
                else:
                    step(ins)
            drained(dve, ("la", 0), ("la", 1))
            dve.wait_ge(dve_step, stepped[0])
            v.scalar_tensor_tensor(gla_av, gla_nv, -1.0, gla_nv, ALU.mult, ALU.max).then_inc(event("gla_abs"), 1)
            conv(2, fms[:, :, :])
            dve.wait_ge(event("gla_log"), 1)
            dve.wait_ge(tab_loaded, 16)
            chain(v.scalar_tensor_tensor(gla_nv, gla_nv, 0.0, gla_av, ALU.max, ALU.add))
            for i in range(GLA_HEADS):
                for c in range(S // CHUNK):
                    at = slice(CHUNK * c, CHUNK * (c + 1))
                    last = step(v.tensor_tensor_scan(gla_bs[:, i, at], tab[:, T_OU:T_OU + CHUNK], gla_nv[:, i, at], 0.0, ALU.mult, ALU.add))
            dve.wait_ge(dve_step, last)
            sums = gla_bs.rearrange("p a (c l) -> p (a c) l", l=CHUNK)
            v.tensor_tensor(gla_av.rearrange("p a (c l) -> p (a c) l", l=CHUNK), sums,
                            sums[:, :, CHUNK - 1:CHUNK].broadcast_to([P, 16, CHUNK]), ALU.subtract).then_inc(event("gla_sums"), 1)
            dense("q")
            dense("k")
            for g in range(2):
                bank = full(dve, ("cbt", g))
                step(v.tensor_tensor(cbt[:, g, 0:S], bank[:, 0:S], tri1, ALU.mult))
                free(v.tensor_tensor(cbt[:, g, S:384], bank[:, S:384], tri1[:, 0:P], ALU.mult), ("cbt", g))
            drained(dve, ("cbt", 0), ("cbt", 1))
            dve.wait_ge(event("gla_exp"), 3)
            drained(dve, ("q", 0), ("q", 1), ("k", 0), ("k", 1))
            step(v.tensor_copy(decay[:, 0:4], gla_eb[:, :, 2 * CHUNK - 1]))
            step(v.tensor_copy(decay[:, 4:8], gla_eb[:, :, 3 * CHUNK - 1]))
            last = step(v.tensor_tensor(q_fm, q_fm, gla_eb, ALU.mult))
            step(v.tensor_tensor(kt[:, :, :], kt[:, :, :], k_fm, ALU.mult))
            chain(v.tensor_tensor(kh[:, :, :], kh[:, :, :], k_fm, ALU.mult))
            step(v.tensor_tensor(k2[:, :, 0:CHUNK], kh[:, :, 0:CHUNK], decay[:, 0:4, None].broadcast_to([P, 4, CHUNK]), ALU.mult))
            step(v.tensor_copy(k2[:, :, CHUNK:P], kh[:, :, CHUNK:P]))
            v.tensor_tensor(q3[:, :, :], q_fm[:, :, 3 * CHUNK:], decay[:, 4:8, None].broadcast_to([P, 4, CHUNK]), ALU.mult)\
                .then_inc(event("gla_operands"), 1)
            dense("v0")
            dense("v1")
            dense("r0")
            dense("r1")
            dve.wait_ge(event("pair_zero"), 1)
            mask = tab[:, T_GLA:T_GLA + P].bitcast(U32)
            for i in range(GLA_HEADS):
                bank = full(dve, ("att", i))
                step(v.copy_predicated(pair[:, i, 0:P], mask, bank[:, 0:P]))
                last = step(v.copy_predicated(pair[:, i, 2 * P:3 * P], mask, bank[:, 2 * P:3 * P]))
                step(v.tensor_copy(pair[:, i, P:2 * P], bank[:, P:2 * P]))
                dve.wait_ge(dve_step, last)
                step(v.tensor_copy(pair[0:CHUNK, i, CHUNK:P], bank[0:CHUNK, 3 * P:3 * P + CHUNK]))
                free(v.tensor_copy(pair[0:CHUNK, i, 2 * P + CHUNK:3 * P], bank[0:CHUNK, 3 * P + CHUNK:4 * P]), ("att", i))
            dense("z0")

            def steps_of(i, f):
                m = steps_mat(i)
                step(v.tensor_scalar(m[:, 0:P], upper, f[:, 0, i:i + 1], None, ALU.mult))
                return v.tensor_scalar(m[:, P:3 * P], ones_upper, f[:, 1, i:i + 1], None, ALU.mult)

            dve.wait_ge(event("dt_done"), 1)
            for i in range(4):
                steps_of(i, da).then_inc(event("ssd_steps"), 1)
            variance("gla", GLA_DV)
            rstd_of("gla")
            for q in range(4):
                t, c = q // 2, q % 2
                for i in range(2):
                    at = slice(512 * c + GLA_DV * i, 512 * c + GLA_DV * (i + 1))
                    ins = v.scalar_tensor_tensor(tme[:, t, at], ps[use["glao", q][0]][:, GLA_DV * i:GLA_DV * (i + 1)],
                                                 rstd[:, 2 * q + i:2 * q + i + 1], silu_r[:, t, at], ALU.mult, ALU.mult)
                    if i == 0:
                        step(ins)
                free(ins, ("glao", q))
            dense("z1")

            for hg in range(4):
                g = hg // 2
                for i in range(4 * hg, 4 * hg + 4):
                    dve.wait_ge(event("ssd_exp"), i + 1)
                    bank = ps[use["ssd_d", i][0]]
                    step(v.scalar_tensor_tensor(pair[:, i % 4, 0:S], bank[:, 0:S], dt[:, 0, i:i + 1], cbt[:, g, 0:S], ALU.mult, ALU.mult))
                    free(v.scalar_tensor_tensor(pair[:, i % 4, S:384], bank[:, S:384], dt[:, 1, i:i + 1], cbt[:, g, S:384],
                                                ALU.mult, ALU.mult), ("ssd_d", i))
                if hg < 3:
                    for i in range(4 * hg + 4, 4 * hg + 8):
                        steps_of(i, da).then_inc(event("ssd_steps"), 1)
                if hg in (1, 2):
                    for q in (2 * hg - 2, 2 * hg - 1):
                        operand(("ygt", q), t2l[:, 2 * q:2 * q + 2, :], t2h[:, 2 * q:2 * q + 2, :], [C_GLAN, C_GLAN + 1])
                dense(("gs0", "gs1", "gg0", "gg1")[hg])
                if hg == 0:
                    dve.wait_ge(event("skip_ready"), 2)
                bank = full(dve, ("ssd_y", hg))
                at = tmc[:, :, S * hg:S * hg + S]
                free(v.tensor_tensor(at, bank[:, :].rearrange("p (t c) -> p t c", t=NT), at, ALU.add), ("ssd_y", hg))
                drained(dve, ("ssd_y", hg))
                v.tensor_tensor(at, at, silu_z[:, :, S * hg:S * hg + S], ALU.mult).then_inc(event("y_gated"), 1)
            dve.wait_ge(event("y_gated"), 4)
            variance("ssd", 512)
            rstd_of("ssd")
            for i in range(4):
                t, g = i // 2, i % 2
                at = tmc[:, t, 512 * g:512 * g + 512]
                v.tensor_scalar(at, at, rstd[:, i:i + 1], None, ALU.mult).then_inc(event("y_normed"), 1)

            def up_gla(c):
                def part(b, key):
                    bank = full(dve, key)
                    k = 4 * c + 2 * b
                    at = gate_g[:, k:k + 2, :]
                    free(v.scalar_tensor_tensor(at, at, 1.0, bank[:, :].rearrange("p (k s) -> p k s", k=2), ALU.add, ALU.mult), key)
                return part

            dense("ugla0", up_gla(0))
            for q in range(4):
                operand(("yst", q), t1l[:, 2 * q:2 * q + 2, :], t1h[:, 2 * q:2 * q + 2, :], [C_SSDN + 2 * q, C_SSDN + 2 * q + 1])
            dense("ugla1", up_gla(1))
            norm_begin(1)
            for c in range(2):
                lo(first[f"ussd{c}"] + RING)
                for b in range(2):
                    key = (f"ussd{c}", b)
                    bank = full(dve, key)
                    k = 4 * c + 2 * b
                    at = gate_s[:, k:k + 2, :]
                    free(v.scalar_tensor_tensor(at, at, 1.0, bank[:, :].rearrange("p (k s) -> p k s", k=2), ALU.add, ALU.mult), key)
                    drained(dve, key, (f"ugla{c}", b))
                    v.tensor_tensor(at, at, gate_g[:, k:k + 2, :], ALU.add).then_inc(event("merged"), 1)
                    his[0] += 1
                    dve.wait_ge(operand_hi, his[0])
                    v.scalar_tensor_tensor(t2l[:, k:k + 2, :], at, 0.5, t2h[:, k:k + 2, :].bitcast(F32), ALU.mult, ALU.subtract)\
                        .then_inc(event("merged_lo"), 1)
                lo(first[f"ussd{c}"] + RING + 1)
            norm_end(1)
            dense("wo0", residual("wo", 0))
            dense("wo1", residual("wo", 1))
            norm_begin(2)
            dense("mk0")
            dense("mk1")
            dense("mv0")
            norm_end(2)
            dense("mv1")
            dense("xq0")
            dense("xq1")

            for i in range(X_HEADS):
                bank = full(dve, ("xs", i))
                chain(v.reduce_max(sm[:, 0, 2 * i:2 * i + 2], bank[:, :].rearrange("p (t m) -> p t m", t=NT), AX.X))
                v.tensor_scalar(sm[:, 1, 2 * i:2 * i + 2], sm[:, 0, 2 * i:2 * i + 2], -(X_DH ** -0.5), None, ALU.mult)\
                    .then_inc(event("soft_max"), 1)
            for i in range(X_HEADS):
                drained(dve, ("xs", i))
                chain(v.reciprocal(sm[:, 3, 2 * i:2 * i + 2], sm[:, 2, 2 * i:2 * i + 2]))
                for t in range(NT):
                    at = tmb[:, t, S * i:S * i + S]
                    v.tensor_scalar(at, at, sm[:, 3, 2 * i + t:2 * i + t + 1], None, ALU.mult).then_inc(event("probs_ready"), 1)
            for i in range(X_HEADS):
                operand(("xov", i), t2l[:, 2 * i:2 * i + 2, :], t2h[:, 2 * i:2 * i + 2, :])
            dense("xo0", residual("xo", 0))
            dense_before_norm("xo1", 3, residual("xo", 1))
            ffn(0, 1.0)
            ffn(1, 0.5)

            lo(first["mdown"] + RING)
            dve.wait_ge(sq_done, STATS.index("mla") + 1)
            chain(v.tensor_scalar(var[:, 4:6], ss[:, 4:6], 1.0 / Q_LORA, EPS, ALU.mult, ALU.add))
            v.tensor_scalar(var[:, 6:8], ss[:, 6:8], 1.0 / KV_LORA, EPS, ALU.mult, ALU.add).then_inc(var_ready, 1)
            rstd_of("mla")
            chain(v.tensor_tensor(scales[:, 4:8].rearrange("p (a t) -> p a t", t=NT), rstd[:, 4:8].rearrange("p (a t) -> p a t", t=NT),
                                  rstd[:, None, 0:2].broadcast_to([P, 2, NT]), ALU.mult))

            def rotate(dst_list, src, t, n, at, last_free=None):
                half = ROPE // 2
                a = tmd[:, t, at:at + n * ROPE].rearrange("p (n e) -> p n e", n=n)
                b = tmd[:, t, at + n * ROPE:at + 2 * n * ROPE].rearrange("p (n e) -> p n e", n=n)
                cosine, sine = (rot[:, w, t:t + 1, :].broadcast_to([P, n, ROPE]) for w in range(2))
                step(v.tensor_tensor(a, src, cosine, ALU.mult))
                step(v.tensor_tensor(b[:, :, 0:half], src[:, :, half:], sine[:, :, 0:half], ALU.mult))
                ins = v.tensor_tensor(b[:, :, half:], src[:, :, 0:half], sine[:, :, half:], ALU.mult)
                if last_free is not None:
                    free(ins, last_free)
                    drained(dve, last_free)
                    dve.wait_ge(dve_step, stepped[0])
                else:
                    chain(ins)
                for dst, name in dst_list:
                    v.tensor_tensor(dst, a, b, ALU.add).then_inc(event(name), 1)

            for t in range(NT):
                bank = full(dve, ("mdown", t))
                v.tensor_scalar(tmd[:, t, 0:Q_LORA], bank[:, 0:Q_LORA], scales[:, 4 + t:5 + t], None, ALU.mult).then_inc(event("latent"), 1)
                v.tensor_scalar(tmd[:, t, Q_LORA:Q_LORA + KV_LORA], bank[:, Q_LORA:Q_LORA + KV_LORA], scales[:, 6 + t:7 + t], None, ALU.mult)\
                    .then_inc(event("latent"), 1)
            operand(("cqt", 0), t2l[:, 0:2, :], t2h[:, 0:2, :], [C_QN, C_QN + 1])
            operand(("cqt", 1), t2l[:, 2:3, :], t2h[:, 2:3, :], [C_KVN])
            lo(first["mdown"] + RING + 1)
            for t in range(NT):
                bank = ps[use["mdown", t][0]]
                scaled = tmd[:, t, D - ROPE:D]
                free(v.tensor_scalar(scaled, bank[:, Q_LORA + KV_LORA:Q_LORA + KV_LORA + ROPE], rstd[:, t:t + 1], None, ALU.mult), ("mdown", t))
                drained(dve, ("mdown", t))
                src = scaled.rearrange("p (n e) -> p n e", n=1)
                rotate([(tmb[:, t, 512 + ROPE * i:512 + ROPE * i + ROPE].rearrange("p (n e) -> p n e", n=1), "k_rotated") for i in range(2)],
                       src, t, 1, 384)
            for gi in range(2):
                lo(first[f"uq{gi}"] + RING)
                bank = full(dve, ("qr", gi))
                for t in range(NT):
                    rotate([(tmb[:, t, S * gi:S * gi + S].rearrange("p (n e) -> p n e", n=4), "q_rotated")],
                           bank[:, t * S:t * S + S].rearrange("p (n e) -> p n e", n=4), t, 4, 512, ("qr", gi) if t else None)
            lo(first["ukv"] + RING)

            def attention(a, mask_at):
                mask = tab[:, mask_at:mask_at + 3 * P]

                def scores(i):
                    bank = full(dve, (f"as{a}", i))
                    free(v.tensor_tensor(pair[:, i % 4, :], bank[:, 0:3 * P], mask, ALU.add), (f"as{a}", i))
                    drained(dve, (f"as{a}", i))
                    step(v.reduce_max(sm[:, 0, 2 * i:2 * i + 1], pair[:, i % 4, 0:P], AX.X))
                    chain(v.reduce_max(sm[:, 0, 2 * i + 1:2 * i + 2], pair[:, i % 4, P:3 * P], AX.X))
                    v.tensor_scalar(sm[:, 1, 2 * i:2 * i + 2], sm[:, 0, 2 * i:2 * i + 2], -1.0, None, ALU.mult)\
                        .then_inc(event("soft_max"), 1)

                def normalise(i):
                    dve.wait_ge(event("soft_exp"), 8 * a + i + 1)
                    chain(v.reciprocal(sm[:, 3, 2 * i:2 * i + 2], sm[:, 2, 2 * i:2 * i + 2]))
                    for t, (c0, c1) in enumerate(((0, P), (P, 3 * P))):
                        at = pair[:, i % 4, c0:c1]
                        v.tensor_scalar(at, at, sm[:, 3, 2 * i + t:2 * i + t + 1], None, ALU.mult).then_inc(event("probs_ready"), 1)

                for i in range(4):
                    scores(i)
                if a == 1:
                    for i in range(4, 8):
                        steps_of(i, ga).then_inc(event("fox_steps"), 1)
                for i in range(4):
                    normalise(i)
                if a == 1:
                    dense("fv0")
                th, tl = (T2, T1)[a]
                for i in range(8):
                    if i + 4 < 8:
                        full(dve, (f"ap{a}", i))
                        scores(i + 4)
                    for j in outputs_after(a, i):
                        operand((f"ao{a}", j), tl[:, j:j + 1, :], th[:, j:j + 1, :])
                    if i + 4 < 8:
                        normalise(i + 4)
                    if a == 1 and i == 3:
                        dense("fv1")

            attention(0, T_CHUNK)
            dense("mo0", residual("mo", 0))
            dense_before_norm("mo1", 6, residual("mo", 1))
            ffn(2, 0.5)

            def ple(l, n, next_norm):
                lo(first[f"pp{l}"] + RING)

                def embed(c):
                    def part(t, key):
                        drained(dve, key)
                        q = 2 * c + t
                        bank = full(dve, (f"pp{l}", q))
                        at = tmd[:, t, 512 * c:512 * c + 512]
                        free(v.scalar_tensor_tensor(at, at, 1.0, bank[:, :], ALU.add, ALU.mult), (f"pp{l}", q))
                        drained(dve, (f"pp{l}", q))
                        dst = h[:, t, 512 * c:512 * c + 512]
                        v.scalar_tensor_tensor(dst, at, 0.5, dst, ALU.mult, ALU.add).then_inc(event("h_embedded"), 1)
                    return part
                dense(f"pg{l}0", embed(0))
                if next_norm is None:
                    dense(f"pg{l}1", embed(1))
                else:
                    dense_before_norm(f"pg{l}1", next_norm, embed(1))

            ple(0, 7, 8)
            ffn(3, 0.5)
            rstd_of("norm9")
            for t in range(NT):
                v.tensor_scalar(diag[:, t * P:(t + 1) * P], ident, rstd[:, t:t + 1], None, ALU.mult).then_inc(event("diag_ready"), 1)
            dve.wait_ge(event("small_hi"), 2)
            v.tensor_tensor(ws_lo[:, :, 0:FOX_HEADS], ws_raw[:, :, 0:FOX_HEADS], ws_hi[:, :, 0:FOX_HEADS].bitcast(F32), ALU.subtract)\
                .then_inc(event("small_lo"), 1)
            lo(first["fq0"] + RING)
            w, av, ln = (dtw[:, i, :, 0:8] for i in (0, 1, 2))
            bank = full(dve, ("small1", 0))
            step(v.scalar_tensor_tensor(w[:, 0, :], bank[:, 0:8], rstd[:, 0:1], bcast[:, 48:56], ALU.mult, ALU.add))
            free(v.scalar_tensor_tensor(w[:, 1, :], bank[:, 8:16], rstd[:, 1:2], bcast[:, 48:56], ALU.mult, ALU.add), ("small1", 0))
            drained(dve, ("small1", 0))
            dve.wait_ge(dve_step, stepped[0])
            v.scalar_tensor_tensor(av, w, -1.0, w, ALU.mult, ALU.max).then_inc(event("fox_abs"), 1)

            def scaled_part(dst, c, scale):
                def part(b, key):
                    bank = full(dve, key)
                    free(v.scalar_tensor_tensor(dst[:, 4 * c + 2 * b:4 * c + 2 * b + 2, :], bank[:, :].rearrange("p (k s) -> p k s", k=2), scale,
                                                row[:, None, :].broadcast_to([P, 2, S]), ALU.mult, ALU.mult), key)
                return part

            drained(dve, ("row", 0))
            for b in range(2):
                scaled_part(fma, 0, FOX_DH ** -0.5)(b, ("fq0", b))
            lo(first["fq0"] + RING + 1)
            dve.wait_ge(event("fox_log"), 1)
            chain(v.scalar_tensor_tensor(ga[:, :, 0:8], w, 0.0, ln, ALU.min, ALU.subtract))
            for i in range(4):
                steps_of(i, ga).then_inc(event("fox_steps"), 1)
            dense("fq1", scaled_part(fma, 1, FOX_DH ** -0.5))
            for c in range(2):
                dense(f"fk{c}", scaled_part(fmb, c, 1.0))
            attention(1, T_CAUSAL)
            dense("fo0", residual("fo", 0))
            dense_before_norm("fo1", 10, residual("fo", 1))
            ffn(4, 0.5)
            ple(1, 11, None)
            dve.wait_ge(row_loaded, 32)
            dve.wait_ge(event("h_embedded"), 7)
            v.tensor_tensor(tmb[:, 0, :], h[:, 0, :], tma[:, 1, :], ALU.mult).then_inc(event("y_gained"), 1)
            mean_squares("final1", h, "ple1")
            v.tensor_tensor(tmb[:, 1, :], h[:, 1, :], tma[:, 1, :], ALU.mult).then_inc(event("y_gained"), 1)
            rstd_of("final1")
            dve.wait_ge(event("y_gained"), 2)
            v.tensor_scalar(tmb[:, 1, :], tmb[:, 1, :], rstd[:, 1:2], None, ALU.mult).then_inc(event("y_out"), 1)

        @block.gpsimd
        def _(pool):
            g = nc.gpsimd
            stepped = [0]

            def chain(ins):
                ins.then_inc(pool_step, 1)
                stepped[0] += 1
                pool.wait_ge(pool_step, stepped[0])

            chain(g.memset(power[:, :], -0.5))
            chain(g.memset(dtw[:, 6, :, :], -1.0))
            g.memset(pair[:, :, :], 0.0).then_inc(event("pair_zero"), 1)

            def angles():
                pool.wait_ge(tab_loaded, 16)
                pool.wait_ge(rest_loaded, 16 * 6)
                ang, turns = rot[:, 0, :, 0:32], rot[:, 0, :, 32:64]
                chain(g.tensor_copy(pos_f[:, :], pos_i[:, :]))
                for t in range(NT):
                    chain(g.tensor_scalar(ang[:, t, :], tab[:, T_FREQ:T_FREQ + 32], pos_f[:, t:t + 1], None, ALU.mult))
                chain(g.tensor_scalar(turns, ang, float(1.0 / (2.0 * np.pi)), MAGIC, ALU.mult, ALU.add))
                chain(g.tensor_scalar(turns, turns, -MAGIC, None, ALU.add))
                for part in TWO_PI:
                    chain(g.tensor_scalar(rot[:, 1, :, 0:32], turns, -part, None, ALU.mult))
                    chain(g.tensor_tensor(ang, ang, rot[:, 1, :, 0:32], ALU.add))
                g.tensor_scalar(ang, ang, -3.1415925, 3.1415925, ALU.max, ALU.min).then_inc(event("angles"), 1)
                pool.wait_ge(event("sines"), 2)
                chain(g.tensor_tensor(ang, rot[:, 1, :, 0:32], rot[:, 1, :, 0:32], ALU.mult))
                chain(g.tensor_scalar(ang, ang, -2.0, 1.0, ALU.mult, ALU.add))
                chain(g.tensor_copy(rot[:, 0, :, 32:64], ang))
                g.tensor_scalar(rot[:, 1, :, 0:32], rot[:, 1, :, 32:64], -1.0, None, ALU.mult).then_inc(event("rotation"), 1)

            def step_sizes():
                u, e, ln, w4, w5 = (dtw[:, i, :, :] for i in (0, 1, 2, 4, 5))
                pool.wait_ge(event("dt_raw"), 1)
                chain(g.tensor_tensor(u, u, bcast[:, None, 0:16].broadcast_to([P, NT, 16]), ALU.add))
                chain(g.tensor_scalar(e, u, 0.0, 2.0, ALU.max, ALU.mult))
                g.tensor_tensor(e, e, u, ALU.subtract).then_inc(event("dt_abs"), 1)
                pool.wait_ge(event("dt_log"), 1)
                chain(g.tensor_scalar(w4, e, 1.0, -1.0, ALU.add, ALU.add))
                chain(g.tensor_scalar(w5, w4, 0.0, None, ALU.is_equal))
                chain(g.tensor_tensor(w4, w4, w5, ALU.add))
                chain(g.tensor_tensor(w4, w4, dtw[:, 6, :, :], ALU.pow))
                chain(g.tensor_tensor(w4, w4, e, ALU.mult))
                chain(g.tensor_tensor(w4, w4, ln, ALU.mult))
                chain(g.tensor_tensor(w5, w5, e, ALU.mult))
                chain(g.tensor_tensor(w4, w4, w5, ALU.add))
                chain(g.tensor_scalar(u, u, 0.0, None, ALU.max))
                chain(g.tensor_tensor(dt[:, :, :], u, w4, ALU.add))
                chain(g.tensor_tensor(da[:, :, :], dt[:, :, :], dtw[:, 7, 0:1, :].broadcast_to([P, NT, 16]), ALU.mult))
                g.tensor_scalar(da[:, :, :], da[:, :, :], -1.0, None, ALU.mult).then_inc(event("dt_done"), 1)

            for k, key in enumerate(STATS):
                a, b = STAT_COLS.get(key, (0, 2))
                if key == "gla":
                    angles()
                    step_sizes()
                if key == "norm4":
                    full(pool, ("norm4", 3))
                    pool.wait_ge(row_loaded, 32)
                    for t in range(NT):
                        g.tensor_tensor(h[:, t, :], h[:, t, :], tma[:, 0, :], ALU.mult).then_inc(event("h_gained"), 1)
                if key == "ssd":
                    full(pool, ("glao", 3))
                    drained(pool, *quad("xt"))
                    for t in range(NT):
                        g.tensor_tensor(tmc[:, t, :].rearrange("p (a e) -> p a e", e=SSD_P), tma[:, t, :].rearrange("p (a e) -> p a e", e=SSD_P),
                                        bcast[:, 32:48, None].broadcast_to([P, SSD_HEADS, SSD_P]), ALU.mult).then_inc(event("skip_ready"), 1)
                pool.wait_ge(var_ready, k + 1)
                g.tensor_tensor(rstd[:, a:b], var[:, a:b], power[:, a:b], ALU.pow).then_inc(rstd_ready, 1)

        @block.tensor
        def _(pe):
            mm, turn = nc.tensor.matmul, nc.tensor.transpose

            def start(key):
                b, i = use[key]
                if i > 0:
                    pe.wait_ge(bank_free[b], i)
                return ps[b]

            def end(ins, key):
                ins.then_inc(bank_full[use[key][0]], 1)

            def product(dst, stationary, moving, first_k, last_k, shared=False):
                (sh, sl), (mh, ml) = stationary, moving
                mm(dst, sh, mh, start=first_k, stop=False, skip_group_check=shared)
                mm(dst, sh, ml, start=False, stop=False, skip_group_check=shared)
                return mm(dst, sl, mh, start=False, stop=last_k, skip_group_check=shared)

            def k_and_t(tiles_apart):
                return [(kk, t) for t in range(NT) for kk in range(4)] if tiles_apart else [(kk, t) for kk in range(4) for t in range(NT)]

            def before(k, ready, hooks):
                if hooks and k in hooks:
                    hooks[k]()
                if ready is not None:
                    ready(k)

            def token_major(name, T, n=512, ready=None, hooks=None):
                th, tl = T
                banks = [start((name, t)) for t in range(NT)]
                for half in range(2):
                    g = first[name] + half
                    pe.wait_ge(w_lo_ready, g + 1)
                    for kk, t in k_and_t(half == 1):
                        k = 4 * half + kk
                        if t == 0:
                            before(k, ready, hooks)
                        w = tuple(x[:, g % RING, kk * n:(kk + 1) * n] for x in (w_hi, w_lo))
                        x = tuple(y[:, k, t * P:(t + 1) * P] for y in (th, tl))
                        ins = product(banks[t][:, 0:n], x, w, k == 0, k == KD - 1)
                        if k == KD - 1:
                            end(ins, (name, t))
                    if half == 0:
                        ins.then_inc(w_used, 1)

            def feature_major(name, T, ready=None, hooks=None):
                th, tl = T
                banks = [start((name, b)) for b in range(2)]
                for half in range(2):
                    g = first[name] + half
                    pe.wait_ge(w_lo_ready, g + 1)
                    for kk, b in k_and_t(half == 1):
                        k = 4 * half + kk
                        if b == 0:
                            before(k, ready, hooks)
                        for f in (2 * b, 2 * b + 1):
                            w = tuple(x[:, g % RING, kk * 512 + f * P:kk * 512 + (f + 1) * P] for x in (w_hi, w_lo))
                            x = (th[:, k, :], tl[:, k, :])
                            ins = product(banks[f // 2][:, (f % 2) * S:(f % 2) * S + S], w, x, k == 0 and f % 2 == 0, k == KD - 1, shared=True)
                            if k == KD - 1 and f % 2:
                                end(ins, (name, f // 2))
                    if half == 0:
                        ins.then_inc(w_used, 1)

            def turn_operand(name, src, qs=range(4)):
                for q in qs:
                    bank = start((name, q))
                    for i in range(4):
                        k, t = 2 * q + i // 2, i % 2
                        ins = turn(bank[:, (i // 2) * S + t * P:(i // 2) * S + (t + 1) * P], src[:, t, k * P:(k + 1) * P], ident)
                    end(ins, (name, q))

            def norm(n):
                pe.wait_ge(xn_ready, 2 * (n + 1))
                turn_operand(f"norm{n}", tme)

            def operand_ready(name):
                drained(pe, *quad(name))

            def tiles_of(name):
                def wait(k):
                    if k % 2 == 0:
                        drained(pe, (name, k // 2))
                return wait

            def turn_half(n, c):
                def turn_now():
                    h_half_ready(pe, UPDATE_BEFORE[n], c)
                    for q in (2 * c, 2 * c + 1):
                        bank = start((f"norm{n}", q))
                        for i in range(4):
                            k, t = 2 * q + i // 2, i % 2
                            ins = turn(bank[:, (i // 2) * S + t * P:(i // 2) * S + (t + 1) * P], h[:, t, k * P:(k + 1) * P], ident)
                        end(ins, (f"norm{n}", q))
                return turn_now

            def ffn(n):
                g0 = first[f"ffn{n}"]
                b0, b1, b2 = (use[k][1] for k in ((f"gu{n}", 0), (f"gu{n}", 1), (f"ht{n}", 0)))
                acc = [ps[4 + q] for q in range(4)]
                n_in, n_out = NORM_OF_FFN[n], NORM_AFTER_FFN[n]
                T, U = T_OF_NORM[n_in], T_OF_HIDDEN[n]

                def gate_up(j, first_block=False, between=None):
                    for half in range(2):
                        c = g0 + half if first_block else g0 - 1 + half
                        slot = c % RING
                        pe.wait_ge(w_lo_ready, c + 1 if first_block else 3 * j + (c + 1))
                        for kk, t in k_and_t(half == 1 or not first_block):
                            k = 4 * half + kk
                            if first_block and t == 0:
                                before(k, tiles_of(f"norm{n_in}"), {2: turn_half(n_in, 1)})
                            if between is not None and k == 0:
                                pe.wait_ge(bank_free[t], (b0, b1)[t] + 1)
                            w = tuple(x[:, slot, kk * 512:(kk + 1) * 512] for x in (w_hi, w_lo))
                            x = tuple(y[:, k, t * P:(t + 1) * P] for y in T)
                            ins = product(ps[t][:, :], x, w, k == 0, k == KD - 1)
                            if k == KD - 1:
                                ins.then_inc(bank_full[t], 1)
                        if half == 0:
                            ins.then_inc(w_used, 1)
                            if between is not None:
                                between()

                def turned(j):
                    pe.wait_ge(bank_free[0], j + (b0 + 1))
                    pe.wait_ge(bank_free[1], j + (b1 + 1))
                    pe.wait_ge(bank_free[2], j + b2)
                    for i in range(4):
                        k, t = i // 2, i % 2
                        ins = turn(ps[2][:, k * S + t * P:k * S + (t + 1) * P], ffn_h[:, t, k * P:(k + 1) * P], ident)
                    ins.then_inc(bank_full[2], 1)

                def down_part(slot, kk, q, at=0, first_k=False, last_k=False):
                    t, c = q % 2, q // 2
                    w = tuple(x[:, slot, kk * D + c * 512:kk * D + (c + 1) * 512] for x in (w_hi, w_lo))
                    x = tuple(y[:, at + kk, t * P:(t + 1) * P] for y in U)
                    return product(acc[q][:, :], x, w, first_k, last_k, shared=True)

                def down(i, slot, is_first=False, between=None):
                    pe.wait_ge(bank_free[2], i + b2)
                    pe.wait_ge(w_lo_ready, 3 * i + (g0 + 2))
                    for kk in range(2):
                        for q in range(4):
                            ins = down_part(slot, kk, q, first_k=is_first and kk == 0)
                        if kk == 0 and between is not None:
                            between()
                    ins.then_inc(w_used, 1)

                pe.wait_ge(bank_free[0], b0)
                pe.wait_ge(bank_free[1], b1)
                gate_up(0, True)

                def first_turned():
                    turned(0)
                    if n in PLE_OF_FFN:
                        l = PLE_OF_FFN[n]
                        bank = start((f"pt{l}", 0))
                        pe.wait_ge(p_loaded, 16 * (l + 1))
                        for i in range(4):
                            k, t = i // 2, i % 2
                            ins = turn(bank[:, k * S + t * P:k * S + (t + 1) * P], fmt[:, t, k * P:(k + 1) * P], ident)
                        end(ins, (f"pt{l}", 0))

                gate_up(1, between=first_turned)
                for q in range(4):
                    start((f"acc{n}", q))
                down(1, (g0 + 4) % RING, is_first=True)
                turned(1)
                with pe.Fori(2, NJ - 1) as i:
                    gate_up(i)
                    down(i, (g0 + 1) % RING)
                    turned(i)
                gate_up(NJ - 1)
                down(NJ - 1, (g0 + 1) % RING, between=lambda: turned(NJ - 1))
                pe.wait_ge(bank_free[2], b2 + NJ)
                pe.wait_ge(w_lo_ready, g0 + 3 * NJ)
                for q in range(4):
                    for kk in range(2):
                        ins = down_part((g0 + 3 * NJ - 1) % RING, kk, q, 4, last_k=kk == 1)
                    end(ins, (f"acc{n}", q))
                    if q == 2:
                        turn_half(n_out, 0)()

            pe.wait_ge(ident_loaded, 16)
            pe.wait_ge(row_mix_loaded, 16)
            end(turn(start(("cols", 0))[:, 0:KD], rows_c[0:KD, :], ident[0:KD, 0:KD]), ("cols", 0))
            norm(0)

            bank = start(("small0", 0))
            pe.wait_ge(event("small_lo"), 1)
            operand_ready("norm0")
            for t in range(NT):
                for k in range(KD):
                    ins = product(bank[:, 32 * t:32 * t + 32], tuple(y[:, k, t * P:(t + 1) * P] for y in T1), (ws_hi[:, k, :], ws_lo[:, k, :]),
                                  k == 0, k == KD - 1)
            end(ins, ("small0", 0))
            bank = start(("a1t", 0))
            drained(pe, ("small0", 0))
            for t in range(NT):
                ins = turn(bank[0:GLA_RANK, t * P:(t + 1) * P], dtw[:, 3, t, :], ident)
            end(ins, ("a1t", 0))
            pe.wait_ge(rows_loaded, 16 * (len(norm_rows) + len(other_rows)))
            n_a = C_CONVW - KD
            end(turn(start(("cols", 1))[:, 0:n_a], rows_a[0:n_a, :], ident[0:n_a, 0:n_a]), ("cols", 1))
            end(turn(start(("cols", 2))[:, 0:n_rows_b], rows_b[0:n_rows_b, :], ident[0:n_rows_b, 0:n_rows_b]), ("cols", 2))
            feature_major("xbc0", T1)
            feature_major("xbc1", T1)
            pe.wait_ge(rest_loaded, 16 * 6)
            drained(pe, ("a1t", 0))
            for i in range(GLA_HEADS):
                key = ("la", i // 2)
                bank = start(key) if i % 2 == 0 else bank
                ins = mm(bank[:, (i % 2) * S:(i % 2) * S + S], wa2[:, i * P:(i + 1) * P], a1t[:, :], start=True, stop=True)
                if i % 2:
                    end(ins, key)
            feature_major("xbc2", T1)
            feature_major("q", T1)
            feature_major("k", T1)

            pe.wait_ge(event("conv_done"), 3)
            pe.wait_ge(tab_loaded, 16)
            for g in range(2):
                bank = start(("cbt", g))
                mm(bank[:, 0:S], fms[:, g, 0:P], fms[:, 2 + g, :], start=True, stop=True)
                end(mm(bank[:, S:384], fms[:, g, P:S], fms[:, 2 + g, P:S], start=True, stop=True), ("cbt", g))
            token_major("v0", T1)
            for q in range(4):
                bank = start(("xt", q))
                t = q // 2
                for i in range(4):
                    ins = turn(bank[:, i * P:(i + 1) * P], x_fm[:, 4 * (q % 2) + i, t * P:(t + 1) * P], ident)
                end(ins, ("xt", q))
            token_major("v1", T1)
            token_major("r0", T1)
            token_major("r1", T1)

            pe.wait_ge(event("gla_operands"), 1)
            for i in range(GLA_HEADS):
                bank = start(("att", i))
                mm(bank[:, 0:P], kt[:, i, 0:P], q_fm[:, i, 0:P], start=True, stop=True)
                mm(bank[:, P:P + CHUNK], k2[:, i, :], q_fm[:, i, P:P + CHUNK], start=True, stop=True)
                mm(bank[:, P + CHUNK:2 * P], k2[:, i, :], q3[:, i, :], start=True, stop=True)
                mm(bank[:, 2 * P:3 * P], kt[:, i, P:S], q_fm[:, i, P:S], start=True, stop=True)
                mm(bank[0:CHUNK, 3 * P:3 * P + CHUNK], kh[:, i, 0:CHUNK], q_fm[:, i, CHUNK:P], start=True, stop=True)
                end(mm(bank[0:CHUNK, 3 * P + CHUNK:4 * P], kh[:, i, P:P + CHUNK], q_fm[:, i, P + CHUNK:S], start=True, stop=True), ("att", i))
            token_major("z0", T1)
            drained(pe, ("v0", 0), ("v0", 1), ("v1", 0), ("v1", 1), *(("att", i) for i in range(4)))
            for q in range(4):
                bank = start(("glao", q))
                t = q // 2
                for i in (2 * (q % 2), 2 * (q % 2) + 1):
                    dst = bank[:, (i % 2) * GLA_DV:(i % 2 + 1) * GLA_DV]
                    at = slice(i * GLA_DV, (i + 1) * GLA_DV)
                    if t == 0:
                        ins = mm(dst, pair[:, i, 0:P], v_tok[:, 0, at], start=True, stop=True)
                    else:
                        mm(dst, pair[:, i, P:2 * P], v_tok[:, 0, at], start=True, stop=False)
                        ins = mm(dst, pair[:, i, 2 * P:3 * P], v_tok[:, 1, at], start=False, stop=True)
                end(ins, ("glao", q))
            token_major("z1", T1)

            for hg in range(4):
                for i in range(4 * hg, 4 * hg + 4):
                    bank = start(("ssd_d", i))
                    pe.wait_ge(event("ssd_steps"), i + 1)
                    m = steps_mat(i)
                    mm(bank[:, 0:S], m[:, 0:P], tri1, start=True, stop=False)
                    mm(bank[:, P:S], m[:, P:2 * P], tri1[:, 0:P], start=False, stop=True)
                    end(mm(bank[:, S:384], m[:, 2 * P:3 * P], tri1[:, 0:P], start=True, stop=True), ("ssd_d", i))
                if hg in (1, 2):
                    operand_ready("glao")
                    turn_operand("ygt", tme, (2 * hg - 2, 2 * hg - 1))
                feature_major(("gs0", "gs1", "gg0", "gg1")[hg], T1)
                drained(pe, *quad("xt"))
                bank = start(("ssd_y", hg))
                drained(pe, *(("ssd_d", i) for i in range(4 * hg, 4 * hg + 4)))
                for i in range(4):
                    at = slice(SSD_P * (4 * hg + i), SSD_P * (4 * hg + i + 1))
                    mm(bank[:, SSD_P * i:SSD_P * (i + 1)], pair[:, i, 0:P], x_tok[:, 0, at], start=True, stop=True)
                    mm(bank[:, S + SSD_P * i:S + SSD_P * (i + 1)], pair[:, i, P:2 * P], x_tok[:, 0, at], start=True, stop=False)
                    ins = mm(bank[:, S + SSD_P * i:S + SSD_P * (i + 1)], pair[:, i, 2 * P:3 * P], x_tok[:, 1, at], start=False, stop=True)
                end(ins, ("ssd_y", hg))
            operand_ready("ygt")
            feature_major("ugla0", T2)
            pe.wait_ge(event("y_normed"), 4)
            turn_operand("yst", tmc)
            feature_major("ugla1", T2)
            operand_ready("yst")
            feature_major("ussd0", T1)
            feature_major("ussd1", T1)
            norm(1)
            token_major("wo0", T2, ready=lambda k: pe.wait_ge(event("merged_lo"), k // 2 + 1))
            token_major("wo1", T2)
            operand_ready("norm1")
            feature_major("mk0", T1)
            feature_major("mk1", T1)
            token_major("mv0", T1)
            norm(2)
            token_major("mv1", T1)
            operand_ready("norm2")
            feature_major("xq0", T2)
            feature_major("xq1", T2)

            drained(pe, *((f"{x}{c}", b) for x in ("mk", "xq", "mv") for c in range(2) for b in range(2)))
            for i in range(X_HEADS):
                bank = start(("xs", i))
                for t in range(NT):
                    for kk in range(2):
                        ins = mm(bank[:, t * S:(t + 1) * S], fma[:, 2 * i + kk, t * P:(t + 1) * P], fmb[:, 2 * i + kk, :], start=kk == 0, stop=kk == 1)
                end(ins, ("xs", i))
            for i in range(X_HEADS):
                bank = start(("xp", i))
                pe.wait_ge(event("probs_ready"), 2 * i + 2)
                for m in range(2):
                    for t in range(NT):
                        ins = turn(bank[:, m * S + t * P:m * S + (t + 1) * P], tmb[:, t, S * i + m * P:S * i + (m + 1) * P], ident)
                end(ins, ("xp", i))
            for i in range(X_HEADS):
                bank = start(("xov", i))
                drained(pe, ("xp", i))
                for j in range(2):
                    for m in range(2):
                        ins = mm(bank[:, j * S:(j + 1) * S], tmc[:, m, X_DH * i + P * j:X_DH * i + P * (j + 1)],
                                 tmd[:, i // 2, 512 * (i % 2) + m * S:512 * (i % 2) + (m + 1) * S], start=m == 0, stop=m == 1)
                end(ins, ("xov", i))
            token_major("xo0", T2, ready=tiles_of("xov"))
            token_major("xo1", T2, hooks={4: turn_half(3, 0)})
            ffn(0)
            ffn(1)

            token_major("mdown", T1, Q_LORA + KV_LORA + ROPE, ready=tiles_of("norm5"), hooks={2: turn_half(5, 1)})
            pe.wait_ge(event("latent"), 4)
            for key, ks in ((("cqt", 0), (0, 1)), (("cqt", 1), (2,))):
                bank = start(key)
                for k in ks:
                    for t in range(NT):
                        ins = turn(bank[:, (k % 2) * S + t * P:(k % 2) * S + (t + 1) * P], tmd[:, t, k * P:(k + 1) * P], ident)
                end(ins, key)
            drained(pe, ("cqt", 0), ("cqt", 1))
            for gi in range(2):
                g = first[f"uq{gi}"]
                pe.wait_ge(w_lo_ready, g + 1)
                w = [x[:, g % RING, 0:2 * 768].rearrange("p (k a e) -> p k a e", k=2, e=NOPE + ROPE) for x in (w_hi, w_lo)]
                bank = start(("qr", gi))
                for t in range(NT):
                    for kk in range(2):
                        ins = product(bank[:, t * S:(t + 1) * S], tuple(y[:, kk, t * P:(t + 1) * P] for y in T2),
                                      tuple(x[:, kk, :, NOPE:] for x in w), kk == 0, kk == 1)
                end(ins, ("qr", gi))
                for i in range(4):
                    key = ("qn", 2 * gi + i // 2)
                    bank = start(key) if i % 2 == 0 else bank
                    for kk in range(2):
                        ins = product(bank[:, (i % 2) * S:(i % 2) * S + S], tuple(x[:, kk, i, 0:NOPE] for x in w),
                                      tuple(y[:, kk, :] for y in T2), kk == 0, kk == 1)
                    if i % 2:
                        end(ins, key)
            g = first["ukv"]
            pe.wait_ge(w_lo_ready, g + 1)
            w = [x[:, g % RING, :].rearrange("p (a e) -> p a e", e=NOPE + 128) for x in (w_hi, w_lo)]
            for i in range(MLA_HEADS):
                key = ("kn", i // 2)
                bank = start(key) if i % 2 == 0 else bank
                ins = product(bank[:, (i % 2) * S:(i % 2) * S + S], tuple(x[:, i, 0:NOPE] for x in w), tuple(y[:, 2, :] for y in T2), True, True)
                if i % 2:
                    end(ins, key)
            for q in range(4):
                bank = start(("kvv", q))
                t, c = q // 2, q % 2
                end(product(bank[:, :], tuple(y[:, 2, t * P:(t + 1) * P] for y in T2), tuple(x[:, 4 * c:4 * c + 4, NOPE:] for x in w), True, True),
                    ("kvv", q))
            pe.wait_ge(event("q_rotated"), 4)
            for q in range(2):
                bank = start(("qrt", q))
                for i in range(4):
                    j, t = i // 2, i % 2
                    ins = turn(bank[:, j * S + t * P:j * S + (t + 1) * P], tmb[:, t, (2 * q + j) * P:(2 * q + j + 1) * P], ident)
                end(ins, ("qrt", q))
            bank = start(("krt", 0))
            pe.wait_ge(event("k_rotated"), 4)
            for t in range(NT):
                ins = turn(bank[:, t * P:(t + 1) * P], tmb[:, t, 512:512 + P], ident)
            end(ins, ("krt", 0))
            drained(pe, ("qrt", 0), ("qrt", 1), ("krt", 0), *quad("qn"), *quad("kn"), *quad("kvv"))

            def attention(a):
                def scores(i):
                    bank = start((f"as{a}", i))
                    if a == 1:
                        pe.wait_ge(event("fox_steps"), i + 1)
                        m = steps_mat(i)
                    half = slice(ROPE * (i % 2), ROPE * (i % 2) + ROPE)
                    for t, c0, keys in ((0, 0, P), (1, P, S)):
                        dst = bank[:, c0:c0 + keys]
                        mm(dst, fma[:, i, t * P:(t + 1) * P], fmb[:, i, 0:keys], start=True, stop=False)
                        if a == 0:
                            ins = mm(dst, fms[half, i // 2, t * P:(t + 1) * P], k_rope[half, 0:keys], start=False, stop=True)
                        elif t == 0:
                            ins = mm(dst, tri1[:, 0:P], m[:, 0:P], start=False, stop=True)
                        else:
                            mm(dst[:, 0:P], tri1[:, P:S], m[:, 0:P], start=False, stop=False)
                            ins = mm(dst, tri1[:, 0:P], m[:, P:3 * P], start=False, stop=True)
                    end(ins, (f"as{a}", i))

                def values(i):
                    drained(pe, (f"ap{a}", i))
                    bank = start((f"ao{a}", i))
                    pt = probs_turned(i)
                    mm(bank[:, 0:S], tmc[:, 0, i * P:(i + 1) * P], pt[:, 0:S], start=True, stop=False)
                    end(mm(bank[:, P:S], tmc[:, 1, i * P:(i + 1) * P], pt[:, S:384], start=False, stop=True), (f"ao{a}", i))

                for i in range(4):
                    scores(i)
                if a == 1:
                    token_major("fv0", T2)
                    drained(pe, ("fv0", 0), ("fv0", 1))
                for i in range(8):
                    bank = start((f"ap{a}", i))
                    pe.wait_ge(event("probs_ready"), 2 * X_HEADS + 16 * a + 2 * i + 2)
                    for c in range(3):
                        ins = turn(bank[:, c * P:(c + 1) * P], pair[:, i % 4, c * P:(c + 1) * P], ident)
                    end(ins, (f"ap{a}", i))
                    if i + 4 < 8:
                        scores(i + 4)
                    for j in outputs_after(a, i):
                        values(j)
                    if a == 1 and i == 3:
                        token_major("fv1", T2)
                        drained(pe, ("fv1", 0), ("fv1", 1))

            def heads_ready(a):
                return lambda k: drained(pe, (f"ao{a}", k))

            attention(0)
            token_major("mo0", T2, ready=heads_ready(0))
            token_major("mo1", T2, hooks={4: turn_half(6, 0)})
            ffn(2)

            def ple(l, n, next_norm):
                T, U = T_OF_NORM[n], T_OF_HIDDEN[2 * l + 2]
                drained(pe, (f"pt{l}", 0))
                g = first[f"pp{l}"]
                pe.wait_ge(w_lo_ready, g + 1)
                banks = [start((f"pp{l}", q)) for q in range(4)]
                for kk in range(2):
                    for q in range(4):
                        t, c = q % 2, q // 2
                        ins = product(banks[q][:, :], tuple(y[:, 2 + kk, t * P:(t + 1) * P] for y in U),
                                      tuple(x[:, g % RING, kk * D + c * 512:kk * D + (c + 1) * 512] for x in (w_hi, w_lo)), kk == 0, kk == 1)
                        if kk == 1:
                            end(ins, (f"pp{l}", q))
                    if kk == 0:
                        turn_half(n, 1)()
                token_major(f"pg{l}0", T, ready=tiles_of(f"norm{n}"))
                token_major(f"pg{l}1", T, hooks={4: turn_half(next_norm, 0)} if next_norm else None)

            ple(0, 7, 8)
            ffn(3)
            feature_major("fq0", T2, ready=tiles_of("norm9"), hooks={2: turn_half(9, 1)})
            bank = start(("small1", 0))
            pe.wait_ge(event("small_lo"), 2)
            for t in range(NT):
                for k in range(KD):
                    ins = product(bank[:, 8 * t:8 * t + 8], tuple(y[:, k, t * P:(t + 1) * P] for y in T2),
                                  (ws_hi[:, k, 0:8], ws_lo[:, k, 0:8]), k == 0, k == KD - 1)
            end(ins, ("small1", 0))
            bank = start(("row", 0))
            pe.wait_ge(event("diag_ready"), 2)
            end(mm(bank[:, 0:S], tri1[:, P:S], diag, start=True, stop=True), ("row", 0))
            for name in ("fq1", "fk0", "fk1"):
                feature_major(name, T2)
            drained(pe, *((f"{x}{c}", b) for x in ("fq", "fk") for c in range(2) for b in range(2)))
            attention(1)
            token_major("fo0", T1, ready=heads_ready(1))
            token_major("fo1", T1, hooks={4: turn_half(10, 0)})
            ffn(4)
            ple(1, 11, None)


_INS = ["x", "mem", "norm_mix", "w_in", "ssd_conv_w", "ssd_conv_b", "ssd_dt_bias", "ssd_A_log", "ssd_D", "ssd_norm",
        "gla_w_a2", "gla_b_a", "gla_norm", "w_up_ssd", "w_up_gla", "w_o", "norm_xattn", "norm_mem", "w_xq", "w_xkv",
        "w_xo", "norm_ffn", "w_ffn_in", "w_ffn_out", "norm_final", "p_2", "positions_2", "ffn_norm_2", "ffn_w_in_2",
        "ffn_w_out_2", "mix_norm_2", "mla_w_down_2", "mla_q_norm_2", "mla_w_uq_2", "mla_kv_norm_2", "mla_w_ukv_2",
        "mla_w_o_2", "fox_w_in_2", "fox_b_f_2", "fox_w_o_2", "ple_norm_2", "ple_w_gate_2", "ple_w_proj_2", "final_norm_2"]


def kernel(**inputs):
    import concourse.bacc as bacc
    from concourse.bass_utils import run_bass_kernel_spmd

    nc = bacc.Bacc("TRN2", target_bir_lowering=False, num_devices=1)
    arrays, aps = {}, {}
    for name, a in [*((n, inputs[n]) for n in _INS), ("tables", tables())]:
        a = np.ascontiguousarray(a)
        arrays[f"in_{name}"] = a
        aps[name] = nc.dram_tensor(f"in_{name}", a.shape, mybir.dt.from_np(a.dtype), kind="ExternalInput").ap()
    out = nc.dram_tensor("out", (1, S, D), F32, kind="ExternalOutput").ap()
    build(nc, aps, out)
    r = run_bass_kernel_spmd(nc, [arrays], core_ids=[0])
    return r.results[0]["out"]
```
